# Optimizing a Trainium2 kernel written in Bass

```python
import jax, jax.numpy as jnp
from jax import lax
import numpy as np
import jax
import jax.numpy as jnp

D_MODEL = 1024
BATCH = 1
SEQ = 512
DEPTH = 2

D_FF = 2816
D_MIX = D_MODEL
HEAD_DIM = 64
N_HEADS = 8
N_KV_HEADS = 2
GROUP = N_HEADS // N_KV_HEADS
ATTN_W = N_HEADS * HEAD_DIM
KV_W = N_KV_HEADS * HEAD_DIM
CONV_CH = D_MIX - ATTN_W
CONV_WIDTH = 31
WINDOW = 128
BLOCK = 128
ROT_DIM = HEAD_DIM // 4
ROPE_THETA = 500000.0
PLE_DIM = 256
EPS = 1e-6
IN_W = ATTN_W + 2 * KV_W + 2 * CONV_CH
SPLITS = (ATTN_W, ATTN_W + KV_W, ATTN_W + 2 * KV_W, ATTN_W + 2 * KV_W + CONV_CH)


def _rms_norm(x, g):
    xf = x.astype(jnp.float32)
    y = xf * lax.rsqrt(jnp.mean(xf * xf, axis=-1, keepdims=True) + EPS)
    return (y * g.astype(jnp.float32)).astype(x.dtype)

def _layer_norm(x, g, b):
    xf = x.astype(jnp.float32)
    mu = jnp.mean(xf, axis=-1, keepdims=True)
    xc = xf - mu
    y = xc * lax.rsqrt(jnp.mean(xc * xc, axis=-1, keepdims=True) + EPS)
    return (y * g.astype(jnp.float32) + b.astype(jnp.float32)).astype(x.dtype)

def _swiglu_ffn(x, w_gate_up, w_down):
    g, u = jnp.split(x @ w_gate_up, 2, axis=-1)
    return (jax.nn.silu(g) * u) @ w_down

def _partial_rope(x, positions):
    half = ROT_DIM // 2
    inv_freq = ROPE_THETA ** (-jnp.arange(0, ROT_DIM, 2, dtype=jnp.float32) / ROT_DIM)
    ang = positions.astype(jnp.float32)[..., None] * inv_freq
    cos = jnp.cos(ang)[:, :, None, :]
    sin = jnp.sin(ang)[:, :, None, :]
    xr = x[..., :ROT_DIM].astype(jnp.float32)
    x1, x2 = xr[..., :half], xr[..., half:]
    rot = jnp.concatenate([x1 * cos - x2 * sin, x2 * cos + x1 * sin], axis=-1).astype(x.dtype)
    return jnp.concatenate([rot, x[..., ROT_DIM:]], axis=-1)

def _sliding_window_attention(q, k, v, sinks):
    B, S, _, hd = q.shape
    nb = S // BLOCK
    qb = q.reshape(B, nb, BLOCK, N_KV_HEADS, GROUP, hd)
    kb = k.reshape(B, nb, BLOCK, N_KV_HEADS, hd)
    vb = v.reshape(B, nb, BLOCK, N_KV_HEADS, hd)
    pad = ((0, 0), (1, 0), (0, 0), (0, 0), (0, 0))
    kk = jnp.concatenate([jnp.pad(kb, pad)[:, :-1], kb], axis=2)
    vv = jnp.concatenate([jnp.pad(vb, pad)[:, :-1], vb], axis=2)
    s = jnp.einsum('bnqkgd,bnskd->bnkgqs', qb, kk).astype(jnp.float32) * (hd ** -0.5)
    qi = jnp.arange(BLOCK)[:, None] + BLOCK
    kj = jnp.arange(2 * BLOCK)[None, :]
    rel = qi - kj
    band = (rel >= 0) & (rel < WINDOW)
    valid = (jnp.arange(nb)[:, None, None] > 0) | (kj[None] >= BLOCK)
    mask = band[None] & valid
    s = jnp.where(mask[None, :, None, None], s, -1e30)
    sink = sinks.astype(jnp.float32).reshape(N_KV_HEADS, GROUP)[None, None, :, :, None, None]
    m = jnp.maximum(jnp.max(s, axis=-1, keepdims=True), sink)
    e = jnp.exp(s - m)
    probs = (e / (jnp.sum(e, axis=-1, keepdims=True) + jnp.exp(sink - m))).astype(v.dtype)
    o = jnp.einsum('bnkgqs,bnskd->bnqkgd', probs, vv)
    return o.reshape(B, S, N_HEADS * hd)

def _conformer_conv(a, g, w_dw, b_dw, ln_g, ln_b):
    u = a * jax.nn.sigmoid(g)
    y = lax.conv_general_dilated(
        u, w_dw[:, None, :].astype(u.dtype), window_strides=(1,),
        padding=[(CONV_WIDTH - 1, 0)],
        dimension_numbers=('NWC', 'WIO', 'NWC'),
        feature_group_count=CONV_CH) + b_dw
    return jax.nn.silu(_layer_norm(y, ln_g, ln_b))

def first_inputs(seed: int = 0) -> dict:
    key = jax.random.key(seed)
    ks = jax.random.split(key, 24)
    f32 = jnp.float32

    def w(k, shape, fan_in, scale=1.0):
        return jax.random.normal(k, shape, f32) * (scale * fan_in ** -0.5)

    def gain(k, shape):
        return 1.0 + 0.02 * jax.random.normal(k, shape, f32)

    L = DEPTH
    x = jax.random.normal(ks[0], (BATCH, SEQ, D_MODEL), f32)
    p = jax.random.normal(ks[1], (DEPTH, BATCH, SEQ, PLE_DIM), f32)
    offsets = jax.random.randint(ks[2], (BATCH, 1), 0, 1024, dtype=jnp.int32)
    positions = offsets + jnp.arange(SEQ, dtype=jnp.int32)[None, :]
    return {
        "x": x,
        "p": p,
        "positions": positions,
        "ffn1_norm": gain(ks[3], (L, D_MODEL)),
        "ffn1_w_gate_up": w(ks[4], (L, D_MODEL, 2 * D_FF), D_MODEL),
        "ffn1_w_down": w(ks[5], (L, D_FF, D_MODEL), D_FF),
        "mix_norm": gain(ks[6], (L, D_MODEL)),
        "w_in": w(ks[7], (L, D_MODEL, IN_W), D_MODEL),
        "sinks": 0.5 * jax.random.normal(ks[8], (L, N_HEADS), f32),
        "conv_w": w(ks[9], (L, CONV_WIDTH, CONV_CH), CONV_WIDTH),
        "conv_b": 0.02 * jax.random.normal(ks[10], (L, CONV_CH), f32),
        "conv_ln_g": gain(ks[11], (L, CONV_CH)),
        "conv_ln_b": 0.02 * jax.random.normal(ks[12], (L, CONV_CH), f32),
        "attn_out_norm": gain(ks[13], (L, ATTN_W)),
        "conv_out_norm": gain(ks[14], (L, CONV_CH)),
        "w_out": w(ks[15], (L, D_MIX, D_MODEL), D_MIX),
        "ffn2_norm": gain(ks[16], (L, D_MODEL)),
        "ffn2_w_gate_up": w(ks[17], (L, D_MODEL, 2 * D_FF), D_MODEL),
        "ffn2_w_down": w(ks[18], (L, D_FF, D_MODEL), D_FF),
        "w_ple": w(ks[19], (L, PLE_DIM, D_MODEL), PLE_DIM),
        "ple_norm": gain(ks[20], (L, D_MODEL)),
        "w_ple_gate": w(ks[21], (L, D_MODEL, D_MODEL), D_MODEL),
        "final_norm": gain(ks[22], (D_MODEL,)),
    }

def first_block(x, p, positions, ffn1_norm, ffn1_w_gate_up, ffn1_w_down, mix_norm, w_in,
              sinks, conv_w, conv_b, conv_ln_g, conv_ln_b, attn_out_norm, conv_out_norm,
              w_out, ffn2_norm, ffn2_w_gate_up, ffn2_w_down, w_ple, ple_norm, w_ple_gate,
              final_norm):
    B, S, _ = x.shape
    h = x
    for i in range(DEPTH):
        h = h + 0.5 * _swiglu_ffn(_rms_norm(h, ffn1_norm[i]), ffn1_w_gate_up[i], ffn1_w_down[i])
        u = _rms_norm(h, mix_norm[i])
        q, k, v, ca, cg = jnp.split(u @ w_in[i], SPLITS, axis=-1)
        q = _partial_rope(q.reshape(B, S, N_HEADS, HEAD_DIM), positions)
        k = _partial_rope(k.reshape(B, S, N_KV_HEADS, HEAD_DIM), positions)
        v = v.reshape(B, S, N_KV_HEADS, HEAD_DIM)
        attn = _sliding_window_attention(q, k, v, sinks[i])
        conv = _conformer_conv(ca, cg, conv_w[i], conv_b[i], conv_ln_g[i], conv_ln_b[i])
        mixed = jnp.concatenate([_rms_norm(attn, attn_out_norm[i]),
                                 _rms_norm(conv, conv_out_norm[i])], axis=-1)
        h = h + mixed @ w_out[i]
        h = h + 0.5 * _swiglu_ffn(_rms_norm(h, ffn2_norm[i]), ffn2_w_gate_up[i], ffn2_w_down[i])
        e = _rms_norm(p[i] @ w_ple[i], ple_norm[i])
        h = h + jax.nn.sigmoid(h @ w_ple_gate[i]) * e
    return _rms_norm(h, final_norm)


N_GDN = 6
N_NSA = 6
N_NSA_KV = 2
NSA_REP = N_NSA // N_NSA_KV
N_SB = 4
D_GDN = N_GDN * HEAD_DIM
D_NSA = N_NSA * HEAD_DIM
D_NSA_KV = N_NSA_KV * HEAD_DIM
D_SB = N_SB * HEAD_DIM
D_MIX_2 = D_GDN + D_NSA + D_SB
GDN_CONV = 4
GDN_CHUNK = 64
CMP_LEN = 32
CMP_STRIDE = 16
CMP_HIDDEN = 128
SEL_BLOCK = 64
SEL_TOPK = 16
WINDOW_2 = 512
Q_BLOCK = 128
FFN_CONV = 3
D_PLE = 256
ROPE_THETA_2 = 10000.0
NEG = -1e30
FORCE_SCORE = 1e4
SPLIT_SIZES = (D_GDN, D_GDN, D_GDN, D_GDN, N_GDN, N_GDN,
               D_NSA, D_NSA_KV, D_NSA_KV, D_NSA_KV, D_NSA_KV, D_NSA_KV, D_NSA_KV, 3 * N_NSA,
               D_SB, D_SB, D_SB)
SPLIT_POINTS = tuple(int(c) for c in np.cumsum(SPLIT_SIZES)[:-1])
N_IN = int(sum(SPLIT_SIZES))


def rmsnorm(x, w):
    xf = x.astype(jnp.float32)
    y = xf * lax.rsqrt(jnp.mean(xf * xf, axis=-1, keepdims=True) + EPS)
    return (y * w.astype(jnp.float32)).astype(x.dtype)

def head_rmsnorm(x, w):
    b, t, c = x.shape
    return rmsnorm(x.reshape(b, t, c // HEAD_DIM, HEAD_DIM), w).reshape(b, t, c)

def l2norm(x):
    return x * lax.rsqrt(jnp.sum(x * x, axis=-1, keepdims=True) + EPS)

def causal_dwconv(x, w):
    k, c = w.shape
    return lax.conv_general_dilated(x, w[:, None, :].astype(x.dtype), window_strides=(1,),
                                    padding=[(k - 1, 0)], dimension_numbers=('NWC', 'WIO', 'NWC'),
                                    feature_group_count=c)

def rope(x, pos):
    half = x.shape[-1] // 2
    inv = ROPE_THETA_2 ** (-jnp.arange(half, dtype=jnp.float32) / half)
    ang = pos.astype(jnp.float32)[..., None] * inv
    cos = jnp.cos(ang)[:, :, None, :]
    sin = jnp.sin(ang)[:, :, None, :]
    xf = x.astype(jnp.float32)
    x1, x2 = xf[..., :half], xf[..., half:]
    return jnp.concatenate([x1 * cos - x2 * sin, x2 * cos + x1 * sin], axis=-1).astype(x.dtype)

def masked_softmax(s, mask):
    s = jnp.where(mask, s, NEG)
    e = jnp.where(mask, jnp.exp(s - jnp.max(s, axis=-1, keepdims=True)), 0.0)
    return e / jnp.maximum(jnp.sum(e, axis=-1, keepdims=True), 1e-30)

def gated_deltanet(q, k, v, z, a, b_logit, conv_w, a_log, dt_bias, norm_w):
    bsz, t, _ = q.shape
    H, D, C = N_GDN, HEAD_DIM, GDN_CHUNK
    n = t // C
    f32 = jnp.float32
    qkv = jax.nn.silu(causal_dwconv(jnp.concatenate([q, k, v], axis=-1), conv_w))
    q, k, v = jnp.split(qkv, 3, axis=-1)
    to_chunks = lambda u_: u_.astype(f32).reshape(bsz, n, C, H, D).transpose(0, 3, 1, 2, 4)
    q = l2norm(to_chunks(q)) * D ** -0.5
    k = l2norm(to_chunks(k))
    v = to_chunks(v)
    beta = jax.nn.sigmoid(b_logit.astype(f32)).reshape(bsz, n, C, H).transpose(0, 3, 1, 2)
    g = -jnp.exp(a_log.astype(f32)) * jax.nn.softplus(a.astype(f32) + dt_bias.astype(f32))
    g = jnp.cumsum(g.reshape(bsz, n, C, H).transpose(0, 3, 1, 2), axis=-1)
    idx = jnp.arange(C)
    incl = idx[:, None] >= idx[None, :]
    strict = idx[:, None] > idx[None, :]
    decay = jnp.exp(jnp.where(incl, g[..., :, None] - g[..., None, :], -jnp.inf))
    k_beta = k * beta[..., None]
    lower = jnp.where(strict, jnp.einsum('bhncd,bhnsd->bhncs', k_beta, k) * decay, 0.0)
    rhs = jnp.concatenate([v * beta[..., None], k_beta * jnp.exp(g)[..., None]], axis=-1)
    sol = lax.linalg.triangular_solve(lower, rhs, left_side=True, lower=True, unit_diagonal=True)
    u, w = jnp.split(sol, 2, axis=-1)
    attn = jnp.einsum('bhncd,bhnsd->bhncs', q, k) * decay

    def step(state, xs):
        q_i, k_i, u_i, w_i, g_i, a_i = xs
        v_new = u_i - jnp.einsum('bhcd,bhde->bhce', w_i, state)
        o_i = (jnp.einsum('bhcd,bhde->bhce', q_i * jnp.exp(g_i)[..., None], state)
               + jnp.einsum('bhcs,bhse->bhce', a_i, v_new))
        g_last = g_i[..., -1:]
        state = (state * jnp.exp(g_last)[..., None]
                 + jnp.einsum('bhcd,bhce->bhde', k_i * jnp.exp(g_last - g_i)[..., None], v_new))
        return state, o_i

    xs = tuple(jnp.moveaxis(t_, 2, 0) for t_ in (q, k, u, w, g, attn))
    _, o = lax.scan(step, jnp.zeros((bsz, H, D, D), f32), xs)
    o = o.transpose(1, 0, 3, 2, 4).reshape(bsz, t, H, D)
    o = rmsnorm(o, norm_w) * jax.nn.silu(z.astype(f32).reshape(bsz, t, H, D))
    return o.reshape(bsz, t, D_GDN).astype(z.dtype)

def compress(kv, pe, w1, w2):
    b, t, g, d = kv.shape
    n_cmp = (t - CMP_LEN) // CMP_STRIDE + 1
    idx = jnp.arange(n_cmp)[:, None] * CMP_STRIDE + jnp.arange(CMP_LEN)[None, :]
    blocks = kv[:, idx] + pe[None, None, :, None, :]
    blocks = blocks.transpose(0, 1, 3, 2, 4).reshape(b, n_cmp, g, CMP_LEN * d)
    return jax.nn.silu(blocks @ w1) @ w2

def native_sparse_attention(q, k_cmp, v_cmp, k_slc, v_slc, k_win, v_win, gates, positions,
                            pe_k, pe_v, ck_w1, ck_w2, cv_w1, cv_w2):
    b, t, _ = q.shape
    G, R, D = N_NSA_KV, NSA_REP, HEAD_DIM
    scale = D ** -0.5
    f32 = jnp.float32
    q = rope(q.reshape(b, t, N_NSA, D), positions).reshape(b, t, G, R, D)
    kv = lambda z_: z_.reshape(b, t, G, D)
    kc = compress(rope(kv(k_cmp), positions), pe_k, ck_w1, ck_w2)
    vc = compress(kv(v_cmp), pe_v, cv_w1, cv_w2)
    n_cmp = kc.shape[1]
    n_sel = t // SEL_BLOCK
    top_k = min(SEL_TOPK, n_sel)
    ks_blk = rope(kv(k_slc), positions).reshape(b, n_sel, SEL_BLOCK, G, D).transpose(0, 3, 1, 2, 4)
    vs_blk = kv(v_slc).reshape(b, n_sel, SEL_BLOCK, G, D).transpose(0, 3, 1, 2, 4)
    pad = ((0, 0), (WINDOW_2, 0), (0, 0), (0, 0))
    kw_pad = jnp.pad(rope(kv(k_win), positions), pad)
    vw_pad = jnp.pad(kv(v_win), pad)
    c0 = jnp.arange(n_cmp) * CMP_STRIDE
    s0 = jnp.arange(n_sel) * SEL_BLOCK
    overlap = jnp.clip(jnp.minimum(c0[:, None] + CMP_LEN, s0[None, :] + SEL_BLOCK)
                       - jnp.maximum(c0[:, None], s0[None, :]), 0).astype(f32) / CMP_LEN
    cmp_end = c0 + CMP_LEN - 1
    b_idx = jnp.arange(b)[:, None, None, None]
    g_idx = jnp.arange(G)[None, :, None, None]
    blk = jnp.arange(n_sel)

    def block(args):
        qb, gb, q0 = args
        tq = q0 + jnp.arange(Q_BLOCK)
        s_c = jnp.einsum('bqgrd,bigd->bgrqi', qb, kc).astype(f32) * scale
        p_c = masked_softmax(s_c, cmp_end[None, :] <= tq[:, None])
        o_c = jnp.einsum('bgrqi,bigd->bqgrd', p_c.astype(vc.dtype), vc)
        imp = jnp.einsum('bgrqi,ij->bgqj', p_c, overlap)
        cur = tq // SEL_BLOCK
        forced = (blk[None, :] == 0) | (blk[None, :] == cur[:, None]) | (blk[None, :] == cur[:, None] - 1)
        visible = blk[None, :] * SEL_BLOCK <= tq[:, None]
        score = jnp.where(forced, FORCE_SCORE, jnp.where(visible, imp, -1.0))
        _, sel = lax.top_k(score, top_k)
        k_sel = ks_blk[b_idx, g_idx, sel].reshape(b, G, Q_BLOCK, top_k * SEL_BLOCK, D)
        v_sel = vs_blk[b_idx, g_idx, sel].reshape(b, G, Q_BLOCK, top_k * SEL_BLOCK, D)
        key_pos = (sel[..., None] * SEL_BLOCK + jnp.arange(SEL_BLOCK)).reshape(b, G, 1, Q_BLOCK, top_k * SEL_BLOCK)
        s_s = jnp.einsum('bqgrd,bgqnd->bgrqn', qb, k_sel).astype(f32) * scale
        p_s = masked_softmax(s_s, key_pos <= tq[:, None])
        o_s = jnp.einsum('bgrqn,bgqnd->bqgrd', p_s.astype(v_sel.dtype), v_sel)
        kw = lax.dynamic_slice_in_dim(kw_pad, q0, WINDOW_2 + Q_BLOCK, axis=1)
        vw = lax.dynamic_slice_in_dim(vw_pad, q0, WINDOW_2 + Q_BLOCK, axis=1)
        pos_w = q0 - WINDOW_2 + jnp.arange(WINDOW_2 + Q_BLOCK)
        diff = tq[:, None] - pos_w[None, :]
        m_w = (diff >= 0) & (diff < WINDOW_2) & (pos_w >= 0)[None, :]
        s_w = jnp.einsum('bqgrd,bngd->bgrqn', qb, kw).astype(f32) * scale
        p_w = masked_softmax(s_w, m_w)
        o_w = jnp.einsum('bgrqn,bngd->bqgrd', p_w.astype(vw.dtype), vw)
        gt = jax.nn.sigmoid(gb.astype(f32))[..., None]
        return (gt[:, :, 0] * o_c + gt[:, :, 1] * o_s + gt[:, :, 2] * o_w).astype(qb.dtype)

    nb = t // Q_BLOCK
    q_blocks = q.reshape(b, nb, Q_BLOCK, G, R, D).transpose(1, 0, 2, 3, 4, 5)
    g_blocks = gates.reshape(b, nb, Q_BLOCK, 3, G, R).transpose(1, 0, 2, 3, 4, 5)
    out = lax.map(block, (q_blocks, g_blocks, jnp.arange(nb) * Q_BLOCK))
    return out.transpose(1, 0, 2, 3, 4, 5).reshape(b, t, D_NSA)

def stick_breaking_attention(q, k, v):
    b, t, _ = q.shape
    H, D = N_SB, HEAD_DIM
    scale = D ** -0.5
    k = k.reshape(b, t, H, D)
    v = v.reshape(b, t, H, D)
    nb = t // Q_BLOCK
    q_blocks = q.reshape(b, nb, Q_BLOCK, H, D).transpose(1, 0, 2, 3, 4)
    key_pos = jnp.arange(t)

    def block(args):
        qb, q0 = args
        tq = q0 + jnp.arange(Q_BLOCK)
        strict = key_pos[None, :] < tq[:, None]
        z = jnp.einsum('bqhd,bkhd->bhqk', qb, k).astype(jnp.float32) * scale
        log_1m = jnp.where(strict, jax.nn.log_sigmoid(-z), 0.0)
        log_stick = lax.cumsum(log_1m, axis=3, reverse=True) - log_1m
        a = jnp.where(strict, jnp.exp(jax.nn.log_sigmoid(z) + log_stick), 0.0)
        return jnp.einsum('bhqk,bkhd->bqhd', a.astype(v.dtype), v)

    out = lax.map(block, (q_blocks, jnp.arange(nb) * Q_BLOCK))
    return out.transpose(1, 0, 2, 3, 4).reshape(b, t, D_SB)

def conv_ffn(x, w_up, conv_w, w_down):
    u = causal_dwconv(x @ w_up, conv_w)
    gate, up = jnp.split(u, 2, axis=-1)
    return (jax.nn.silu(gate) * up) @ w_down

def second_inputs(seed: int = 0) -> dict:
    key = jax.random.key(seed)
    keys = iter(jax.random.split(key, 40))
    f32 = jnp.float32

    def normal(shape, scale):
        return jax.random.normal(next(keys), shape, f32) * scale

    def gain(shape):
        return 1.0 + 0.01 * jax.random.normal(next(keys), shape, f32)

    x = normal((BATCH, SEQ, D_MODEL), 1.0)
    p = normal((DEPTH, BATCH, SEQ, D_PLE), 1.0)
    positions = (jax.random.randint(next(keys), (BATCH, 1), 0, 1024, jnp.int32)
                 + jnp.arange(SEQ, dtype=jnp.int32)[None, :])
    a_log = jnp.log(jax.random.uniform(next(keys), (DEPTH, N_GDN), f32, 1.0, 16.0))
    dt = jnp.exp(jax.random.uniform(next(keys), (DEPTH, N_GDN), f32, -6.907755, -2.302585))
    dt_bias = dt + jnp.log(-jnp.expm1(-dt))
    return {
        'x': x,
        'p': p,
        'positions': positions,
        'ln_mix': gain((DEPTH, D_MODEL)),
        'w_in': normal((DEPTH, D_MODEL, N_IN), D_MODEL ** -0.5),
        'gdn_conv': normal((DEPTH, GDN_CONV, 3 * D_GDN), GDN_CONV ** -0.5),
        'gdn_a_log': a_log,
        'gdn_dt_bias': dt_bias,
        'gdn_norm': gain((DEPTH, HEAD_DIM)),
        'nsa_pe_k': normal((DEPTH, CMP_LEN, HEAD_DIM), 0.1),
        'nsa_pe_v': normal((DEPTH, CMP_LEN, HEAD_DIM), 0.1),
        'nsa_cmp_k_w1': normal((DEPTH, CMP_LEN * HEAD_DIM, CMP_HIDDEN), (CMP_LEN * HEAD_DIM) ** -0.5),
        'nsa_cmp_k_w2': normal((DEPTH, CMP_HIDDEN, HEAD_DIM), CMP_HIDDEN ** -0.5),
        'nsa_cmp_v_w1': normal((DEPTH, CMP_LEN * HEAD_DIM, CMP_HIDDEN), (CMP_LEN * HEAD_DIM) ** -0.5),
        'nsa_cmp_v_w2': normal((DEPTH, CMP_HIDDEN, HEAD_DIM), CMP_HIDDEN ** -0.5),
        'nsa_norm': gain((DEPTH, HEAD_DIM)),
        'sb_norm': gain((DEPTH, HEAD_DIM)),
        'w_out': normal((DEPTH, D_MIX_2, D_MODEL), D_MIX_2 ** -0.5),
        'ln_ffn': gain((DEPTH, D_MODEL)),
        'w_up': normal((DEPTH, D_MODEL, 2 * D_FF), D_MODEL ** -0.5),
        'ffn_conv': normal((DEPTH, FFN_CONV, 2 * D_FF), FFN_CONV ** -0.5),
        'w_down': normal((DEPTH, D_FF, D_MODEL), D_FF ** -0.5),
        'ln_ple': gain((DEPTH, D_MODEL)),
        'w_ple_gate': normal((DEPTH, D_MODEL, D_MODEL), D_MODEL ** -0.5),
        'w_ple': normal((DEPTH, D_PLE, D_MODEL), D_PLE ** -0.5),
        'ple_norm': gain((DEPTH, D_MODEL)),
        'ln_final': gain((D_MODEL,)),
    }

def second_block(x, p, positions, ln_mix, w_in, gdn_conv, gdn_a_log, gdn_dt_bias, gdn_norm,
              nsa_pe_k, nsa_pe_v, nsa_cmp_k_w1, nsa_cmp_k_w2, nsa_cmp_v_w1, nsa_cmp_v_w2,
              nsa_norm, sb_norm, w_out, ln_ffn, w_up, ffn_conv, w_down,
              ln_ple, w_ple_gate, w_ple, ple_norm, ln_final):
    h = x
    for i in range(DEPTH):
        hn = rmsnorm(h, ln_mix[i])
        (g_q, g_k, g_v, g_z, g_a, g_b,
         n_q, n_kc, n_vc, n_ks, n_vs, n_kw, n_vw, n_gate,
         s_q, s_k, s_v) = jnp.split(hn @ w_in[i], SPLIT_POINTS, axis=-1)
        o_gdn = gated_deltanet(g_q, g_k, g_v, g_z, g_a, g_b, gdn_conv[i], gdn_a_log[i],
                               gdn_dt_bias[i], gdn_norm[i])
        o_nsa = native_sparse_attention(n_q, n_kc, n_vc, n_ks, n_vs, n_kw, n_vw, n_gate, positions,
                                        nsa_pe_k[i], nsa_pe_v[i], nsa_cmp_k_w1[i], nsa_cmp_k_w2[i],
                                        nsa_cmp_v_w1[i], nsa_cmp_v_w2[i])
        o_sb = stick_breaking_attention(s_q, s_k, s_v)
        mix = jnp.concatenate([o_gdn, head_rmsnorm(o_nsa, nsa_norm[i]), head_rmsnorm(o_sb, sb_norm[i])], axis=-1)
        h = h + mix @ w_out[i]
        h = h + conv_ffn(rmsnorm(h, ln_ffn[i]), w_up[i], ffn_conv[i], w_down[i])
        gate = jax.nn.sigmoid(rmsnorm(h, ln_ple[i]) @ w_ple_gate[i])
        h = h + gate * rmsnorm(p[i] @ w_ple[i], ple_norm[i])
    return rmsnorm(h, ln_final)


def setup_inputs(seed=0):
    out = dict(first_inputs(seed))
    for name, value in second_inputs(seed + 1).items():
        if name != "x":
            out[name + "_2"] = value
    return out


def reference(
    x, p, positions, ffn1_norm, ffn1_w_gate_up, ffn1_w_down, mix_norm, w_in, sinks, conv_w,
    conv_b, conv_ln_g, conv_ln_b, attn_out_norm, conv_out_norm, w_out, ffn2_norm,
    ffn2_w_gate_up, ffn2_w_down, w_ple, ple_norm, w_ple_gate, final_norm, p_2, positions_2,
    ln_mix_2, w_in_2, gdn_conv_2, gdn_a_log_2, gdn_dt_bias_2, gdn_norm_2, nsa_pe_k_2,
    nsa_pe_v_2, nsa_cmp_k_w1_2, nsa_cmp_k_w2_2, nsa_cmp_v_w1_2, nsa_cmp_v_w2_2, nsa_norm_2,
    sb_norm_2, w_out_2, ln_ffn_2, w_up_2, ffn_conv_2, w_down_2, ln_ple_2, w_ple_gate_2, w_ple_2,
    ple_norm_2, ln_final_2,
):
    x = first_block(
        x, p, positions, ffn1_norm, ffn1_w_gate_up, ffn1_w_down, mix_norm, w_in, sinks, conv_w,
        conv_b, conv_ln_g, conv_ln_b, attn_out_norm, conv_out_norm, w_out, ffn2_norm,
        ffn2_w_gate_up, ffn2_w_down, w_ple, ple_norm, w_ple_gate, final_norm,
    )
    return second_block(
        x, p_2, positions_2, ln_mix_2, w_in_2, gdn_conv_2, gdn_a_log_2, gdn_dt_bias_2,
        gdn_norm_2, nsa_pe_k_2, nsa_pe_v_2, nsa_cmp_k_w1_2, nsa_cmp_k_w2_2, nsa_cmp_v_w1_2,
        nsa_cmp_v_w2_2, nsa_norm_2, sb_norm_2, w_out_2, ln_ffn_2, w_up_2, ffn_conv_2, w_down_2,
        ln_ple_2, w_ple_gate_2, w_ple_2, ple_norm_2, ln_final_2,
    )


_drawn_inputs = setup_inputs


def setup_inputs(seed=0):
    import zlib

    import numpy as np

    out = dict(_drawn_inputs(seed))
    spreads = {}
    factors = {'ffn1_norm': 4.172,
     'attn_out_norm': 2.839,
     'conv_out_norm': 3.582,
     'ffn2_norm': 6.932,
     'ple_norm': 5.36,
     'ln_mix_2': 4.817,
     'gdn_norm_2': 24.156,
     'nsa_pe_k_2': 8.0,
     'nsa_norm_2': 64.0,
     'sb_norm_2': 64.0,
     'ln_ffn_2': 7.29,
     'ln_ple_2': 64.0,
     'ple_norm_2': 180.542,
     'ln_final_2': 167.247,
     'nsa_pe_v_2': 7.651}
    for name, (base, spread) in spreads.items():
        noise = np.random.default_rng([zlib.crc32(name.encode()), seed]).standard_normal(out[name].shape)
        drawn = base * np.exp(spread * noise) if base else spread * noise
        out[name] = jnp.asarray(drawn.astype(out[name].dtype))
    for name, factor in factors.items():
        out[name] = (out[name] * factor).astype(out[name].dtype)
    return out
```

```python
from contextlib import ExitStack, contextmanager

import numpy as np
import concourse.bass as bass
from concourse import mybir

F32 = mybir.dt.float32
F32R = mybir.dt.float32r
I32 = mybir.dt.int32
ACT = mybir.ActivationFunctionType
ALU = mybir.AluOpType
AX_X = mybir.AxisListType.X

P = 128
T = 512
NB = T // P
D = 1024
DC = D // P
FF = 2816
FC = FF // P
HD = 64
DEPTH = 2
EPS = 1e-6
NEG = -1e30
GROUPS = [8, 8, FC - 16]
UW = DC * P
FFN_UNITS = sum(2 * g + DC for g in GROUPS)

GT = 3
LEVELS = 6
NCMP = 31
HN, HS = 6, 4
IN2 = ([("rows", 0)] + [("conv", n) for n in range(9)] + [("z", n) for n in range(3)]
       + [("rope", 0), ("vc", 0), ("rope", 1), ("tok", 0), ("rope", 2), ("tok", 1)]
       + [("rope", 3 + n) for n in range(3)] + [("sq", 0), ("sq", 1), ("sk", 0), ("sk", 1), ("tok", 2), ("tok", 3)])
U2_PLE = len(IN2)
U2_OUT = U2_PLE + 2
U2_FFN = U2_OUT + DC
U2_GATE = U2_FFN + FFN_UNITS
U2 = U2_GATE + DC

H1, KV1 = 8, 2
TAPS = 31
CT = 4
U1_IN = FFN_UNITS
U1_PLE = U1_IN + 14
U1_OUT = U1_PLE + 2
U1_FFN2 = U1_OUT + DC
U1_GATE = U1_FFN2 + FFN_UNITS
U1 = U1_GATE + DC


class Count:

    def __init__(self):
        self.count = {}

    def up(self, name):
        self.count[name] = self.count.get(name, 0) + 1
        return self.count[name]

    @contextmanager
    def turns(self, i, n, per_turn):
        base = {k: self.count.get(k, 0) for k in per_turn}
        for k, m in per_turn.items():
            self.count[k] = i * m + base[k]
        yield
        for k, m in per_turn.items():
            self.count[k] = base[k] + n * m


def due(value):
    return not isinstance(value, int) or value > 0


class Layout:

    def __init__(self, nc, start, size):
        self.nc, self.at, self.end = nc, start, start + size

    def __call__(self, name, shape, dt=F32):
        size = 4 * int(np.prod(shape[1:]))
        t = self.nc.alloc_sbuf_tensor_at(name, shape, dt, offset=self.at)
        self.at += (size + 31) // 32 * 32
        assert self.at <= self.end, (name, self.at, self.end)
        return t


CONST = {}


def const_columns():
    q = np.arange(P)
    parts = {}
    parts["ident"] = np.eye(P)
    parts["eps"] = np.full((P, 1), EPS)
    parts["mean_d"] = np.full((P, P), 1.0 / D)
    parts["mean_c"] = np.full((P, P), 1.0 / 512)
    causal = np.where(q[None, :] <= q[:, None], 0.0, NEG)
    parts["band"] = np.concatenate([np.where(q[None, :] > q[:, None], 0.0, NEG), causal], 1)
    r = q % HD
    partner = np.where(r < 8, q + 8, np.where(r < 16, q - 8, q))
    parts["swap1"] = (q[:, None] == partner[None, :]) * 1.0
    f = np.float32(500000.0) ** (-np.arange(0, 16, 2, dtype=np.float32) / np.float32(16))
    parts["freq1"] = np.where(r < 16, f[r % 8], 0.0)[:, None]
    parts["sign1"] = np.where(r < 8, -1.0, np.where(r < 16, 1.0, 0.0))[:, None]
    r2 = q % HD
    parts["swap2"] = (q[:, None] == np.where(r2 < 32, q + 32, q - 32)[None, :]) * 1.0
    f2 = np.float32(10000.0) ** (-np.arange(32, dtype=np.float32) / np.float32(32))
    parts["freq2"] = f2[r2 % 32][:, None]
    parts["sign2"] = np.where(r2 < 32, -1.0, 1.0)[:, None]
    parts["head_sum"] = (q[:, None] // HD == q[None, :] // HD) * 1.0
    parts["causal"] = causal
    parts["seen"] = np.tile(np.where(q[:, None] <= q[None, :], 0.0, NEG), (1, NB))
    parts["before"] = np.where(q[:, None] < q[None, :], 0.0, NEG)
    parts["neg_tri"] = np.where(q[:, None] >= q[None, :], -1.0, 0.0)
    parts["neg_one"] = np.full((P, P), -1.0)
    parts["pick"] = np.concatenate([np.repeat((q % 32 == h)[:, None] * 1.0, P, 1) for h in range(6)], 1)
    parts["pick2"] = np.concatenate([(q[:, None] % 32 == 2 * t + q[None, :] // HD) * 1.0 for t in range(3)], 1)
    for n in range(LEVELS + 1):
        s = 2 ** n
        parts[f"level{n}"] = ((q[:, None] // (2 * s) == q[None, :] // (2 * s)) & (q[:, None] // s % 2 == 0)
                              & (q[None, :] // s % 2 == 1)) * 1.0
    tok = q[:, None] + P * np.arange(NB)[None, :]
    parts["cmp_mask"] = np.where(16 * np.arange(NCMP)[None, None, :] + 31 <= tok[:, :, None], 0.0, NEG).reshape(P, -1)
    parts["cmp_any"] = (tok >= 31) * 1.0
    for g in range(2):
        parts[f"both{g}"] = (q[:, None] == g * HD + q[None, :] % HD) * 1.0
    at, cols = {}, 0
    for k, v in parts.items():
        at[k] = (cols, v.shape[1])
        cols += v.shape[1]
    return at, np.concatenate(list(parts.values()), 1).astype(np.float32)


SMALL1 = {}
_n = 0
for _k, _w in [("ffn1", 8), ("mix", 8), ("ffn2", 8), ("ple", 8), ("ln_g", 4), ("ln_b", 4), ("conv_b", 4),
               ("conv_out", 4), ("taps", 4 * TAPS), ("sinks", 8), ("attn_out", 512)]:
    SMALL1[_k] = (_n, _w)
    _n += _w
NS1 = _n


SMALL2 = {}
_n = 0
for _k, _w in [("mix", 8), ("ffn", 8), ("gate", 8), ("ple", 8), ("conv", 36), ("fconv", 132), ("a_log", 1), ("dt", 1),
               ("gdn_norm", 64), ("nsa_norm", 64), ("sb_norm", 64), ("pe_k", 16), ("pe_v", 16), ("w2_k", 64),
               ("w2_v", 64)]:
    SMALL2[_k] = (_n, _w)
    _n += _w
NS2 = _n


def build(nc, io, which):
    with ExitStack() as ctx:
        base = -(-nc.sbuf_base // 64) * 64
        room = nc.sbuf_bytes_remaining
        ctx.enter_context(nc.sbuf_tensor("arena", [P, room // 4 - 48], F32))
        sb = Layout(nc, base, room - 256)
        at, table = const_columns()
        NCONST = table.shape[1]
        h = sb("h", [P, DC, T])
        x_at = sb.at
        xh = sb("xh", [P, DC, T], F32R)
        xl = sb("xl", [P, DC, T], F32R)
        f_at = sb.at
        fh = sb("fh", [P, 8, T], F32R)
        fl = sb("fl", [P, 8, T], F32R)
        raw = [sb(f"raw{k}", [P, UW]) for k in range(4)]
        wh = [sb(f"wh{k}", [P, UW], F32R) for k in range(2)]
        wl = [sb(f"wl{k}", [P, UW], F32R) for k in range(2)]
        con = sb("con", [P, NCONST])
        cos = sb("cos", [P, T])
        sin = sb("sin", [P, T])
        rstd = sb("rstd", [P, T])
        gbuf_at = sb.at
        gbuf = sb("gbuf", [P, T])
        ubuf = sb("ubuf", [P, T])
        sbuf = sb("sbuf", [P, T])
        fbuf = sb("fbuf", [P, T])
        sq = sb("sq", [P, 2, T])
        e_at = sb.at
        e_t = sb("e_t", [P, DC, T])
        mix_at = sb.at

        def c(name):
            a, n = at[name]
            return con[:, a:a + n]

        ps = [ctx.enter_context(nc.psum_tensor(f"ps{k}", [P, 512], F32)) for k in range(8)]
        DB, STAT, BK = ps[0:2], ps[2], ps[3:8]

        def start_block(first, sems):
            with ExitStack() as own:
                s = {n: own.enter_context(nc.semaphore(n)) for n in ["start_in", "start_dve", "start_act"]}
                ids = [v.num for v in s.values()]
                tb = Layout(nc, f_at, 32768)
                pre = "a" if first else "b"
                posi = tb(f"posi{pre}", [P, T], I32)
                ang, turn, red = tb(f"ang{pre}", [P, T]), tb(f"turn{pre}", [P, T]), tb(f"red{pre}", [P, T])
                k = "1" if first else "2"
                with nc.Block() as block:
                    @block.sync
                    def _(sp):
                        n = 2
                        sp.dma_start(posi[:, :], io["pos" + k]).then_inc(s["start_in"], 16)
                        sp.dma_start(con[:, :], io["consts"]).then_inc(s["start_in"], 16)
                        if first or which == 2:
                            sp.dma_start(h[:, :, :], io["x"]).then_inc(s["start_in"], 16)
                            n = 3
                        sp.wait_ge(s["start_in"], 16 * n)

                    @block.vector
                    def _(dve):
                        st = Count()
                        v = nc.vector
                        dve.wait_ge(s["start_in"], 48 if (first or which == 2) else 32)
                        v.tensor_copy(turn[:, :], posi[:, :]).then_inc(s["start_dve"], 1)
                        dve.wait_ge(s["start_dve"], st.up("start_dve"))
                        v.tensor_scalar(ang[:, :], turn[:, :], c("freq" + k), None, ALU.mult)\
                            .then_inc(s["start_dve"], 1)
                        dve.wait_ge(s["start_dve"], st.up("start_dve"))
                        two_pi = 2 * np.pi
                        c1 = 6.28125
                        c2 = float(np.float32(np.round((two_pi - c1) * 2.0 ** 20) / 2.0 ** 20))
                        c3 = two_pi - c1 - c2
                        magic = 1.5 * 2.0 ** 23
                        for out, quarter in ((sin, 0.0), (cos, 0.25)):
                            v.tensor_scalar(turn[:, :], ang[:, :], 1 / two_pi, quarter, ALU.mult, ALU.add)\
                                .then_inc(s["start_dve"], 1)
                            dve.wait_ge(s["start_dve"], st.up("start_dve"))
                            v.tensor_scalar(turn[:, :], turn[:, :], magic, None, ALU.add).then_inc(s["start_dve"], 1)
                            dve.wait_ge(s["start_dve"], st.up("start_dve"))
                            v.tensor_scalar(turn[:, :], turn[:, :], -magic, None, ALU.add).then_inc(s["start_dve"], 1)
                            dve.wait_ge(s["start_dve"], st.up("start_dve"))
                            v.scalar_tensor_tensor(red[:, :], turn[:, :], -c1, ang[:, :], ALU.mult, ALU.add)\
                                .then_inc(s["start_dve"], 1)
                            dve.wait_ge(s["start_dve"], st.up("start_dve"))
                            v.scalar_tensor_tensor(red[:, :], turn[:, :], -c2, red[:, :], ALU.mult, ALU.add)\
                                .then_inc(s["start_dve"], 1)
                            dve.wait_ge(s["start_dve"], st.up("start_dve"))
                            v.scalar_tensor_tensor(red[:, :], turn[:, :], -c3, red[:, :], ALU.mult, ALU.add)\
                                .then_inc(s["start_dve"], 1)
                            dve.wait_ge(s["start_dve"], st.up("start_dve"))
                            v.tensor_scalar(red[:, :], red[:, :], quarter * two_pi, 3.1415925, ALU.add, ALU.min)\
                                .then_inc(s["start_dve"], 1)
                            dve.wait_ge(s["start_dve"], st.up("start_dve"))
                            v.tensor_scalar(out[:, :], red[:, :], -3.1415925, None, ALU.max)\
                                .then_inc(s["start_dve"], 1)
                            dve.wait_ge(s["start_dve"], st.up("start_dve"))
                        ready = st.count["start_dve"]
                        assert ready == 18
                        dve.wait_ge(s["start_act"], 2)
                        v.tensor_scalar(sin[:, :], sin[:, :], c("sign" + k), None, ALU.mult)\
                            .then_inc(s["start_dve"], 1)
                        dve.wait_ge(s["start_dve"], st.up("start_dve"))

                    @block.scalar
                    def _(act):
                        st = Count()
                        act.wait_ge(s["start_dve"], 18)
                        nc.scalar.activation(sin[:, :], sin[:, :], ACT.Sin).then_inc(s["start_act"], 1)
                        act.wait_ge(s["start_act"], st.up("start_act"))
                        nc.scalar.activation(cos[:, :], cos[:, :], ACT.Sin).then_inc(s["start_act"], 1)
                        act.wait_ge(s["start_act"], st.up("start_act"))
                nc.gpsimd.sem_clear(range(min(ids), max(ids) + 1))
                nc.all_engine_barrier()

        def final_norm(gain, out):
            with ExitStack() as own:
                s = {n: own.enter_context(nc.semaphore(n)) for n in ["gain_in", "fin_sq", "fin_sum", "fin_dve", "fin_out"]}
                ids = [v.num for v in s.values()]
                gcol = Layout(nc, f_at, 32768)("gcol" + gain, [P, DC])
                with nc.Block() as block:
                    @block.sync
                    def _(sp):
                        sp.dma_start(gcol[:, :], io[gain]).then_inc(s["gain_in"], 16)
                        if out is not None:
                            for j in range(DC):
                                sp.wait_ge(s["fin_dve"], j + 2)
                                sp.dma_start(out[:, j], h[:, j, :]).then_inc(s["fin_out"], 16)
                            sp.wait_ge(s["fin_out"], 16 * DC)

                    @block.scalar
                    def _(act):
                        st = Count()
                        for j in range(DC):
                            if due(j - 1):
                                act.wait_ge(s["fin_sum"], j - 1)
                            nc.scalar.activation(sq[:, j % 2, :], h[:, j, :], ACT.Square).then_inc(s["fin_sq"], 1)
                            act.wait_ge(s["fin_sq"], st.up("fin_sq"))
                        act.wait_ge(s["fin_sum"], DC)
                        nc.scalar.activation(rstd[:, :], STAT[:, :], ACT.Sqrt, bias=c("eps")).then_inc(s["fin_sq"], 1)
                        act.wait_ge(s["fin_sq"], st.up("fin_sq"))

                    @block.tensor
                    def _(pe):
                        for j in range(DC):
                            pe.wait_ge(s["fin_sq"], j + 1)
                            nc.tensor.matmul(STAT[:, :], c("mean_d"), sq[:, j % 2, :], start=(j == 0),
                                             stop=(j == DC - 1)).then_inc(s["fin_sum"], 1)

                    @block.vector
                    def _(dve):
                        st = Count()
                        dve.wait_ge(s["gain_in"], 16)
                        dve.wait_ge(s["fin_sq"], DC + 1)
                        nc.vector.reciprocal(rstd[:, :], rstd[:, :]).then_inc(s["fin_dve"], 1)
                        dve.wait_ge(s["fin_dve"], st.up("fin_dve"))
                        for j in range(DC):
                            nc.vector.scalar_tensor_tensor(h[:, j, :], h[:, j, :], gcol[:, j:j + 1],
                                                           rstd[:, :], ALU.mult, ALU.mult).then_inc(s["fin_dve"], 1)
                            dve.wait_ge(s["fin_dve"], st.up("fin_dve"))
                nc.gpsimd.sem_clear(range(min(ids), max(ids) + 1))
                nc.all_engine_barrier()

        COMMON = ["raw0", "raw1", "raw2", "raw3", "w_hi", "w_lo", "unit", "bank", "x_hi", "x_lo",
                  "sq_done", "sq_sum", "stat_read", "act_step", "dve_step", "silu", "ff", "ff_hi", "ff_lo",
                  "small_in"]

        def sp_weights(sp, s, stream, n):
            for u in range(4):
                sp.dma_start(raw[u][:, :], stream[u]).then_inc(s[f"raw{u}"], 16)
            with sp.Fori(1, n // 4) as i:
                for k in range(4):
                    sp.wait_ge(s["w_lo"], i * 4 + (k - 3))
                    sp.dma_start(raw[k][:, :], stream[i * 4 + k]).then_inc(s[f"raw{k}"], 16)
            for u in range(n // 4 * 4, n):
                sp.wait_ge(s["w_lo"], u - 3)
                sp.dma_start(raw[u % 4][:, :], stream[u]).then_inc(s[f"raw{u % 4}"], 16)

        def act_split(act, s, st, i, k):
            act.wait_ge(s[f"raw{k % 4}"], i * 16 + 16 * (k // 4 + 1))
            if due(i * 4 + (k - 1)):
                act.wait_ge(s["unit"], i * 4 + (k - 1))
            nc.scalar.activation(wh[k % 2][:, :], raw[k % 4][:, :], ACT.Copy).then_inc(s["w_hi"], 1)
            act.wait_ge(s["w_hi"], st.up("w_hi"))

        def dve_split(dve, s, st, i, k):
            dve.wait_ge(s["w_hi"], i * 4 + (k + 1))
            nc.vector.tensor_tensor(wl[k % 2][:, :], raw[k % 4][:, :], wh[k % 2][:, :].bitcast(F32),
                                    ALU.subtract).then_inc(s["w_lo"], 1)
            dve.wait_ge(s["w_lo"], st.up("w_lo"))

        def pe_unit(pe, s, i, k, hi, lo, n=DC, chunk_waits=None):
            pe.wait_ge(s["w_lo"], i * 4 + (k + 1))
            if due(i * 4 + (k - 1)):
                pe.wait_ge(s["bank"], i * 4 + (k - 1))
            for q in range(n):
                if chunk_waits:
                    name, value = chunk_waits(q)
                    pe.wait_ge(s[name], value)
                a, b = wh[k % 2][:, q * P:(q + 1) * P], wl[k % 2][:, q * P:(q + 1) * P]
                nc.tensor.matmul(DB[k % 2][:, :], a, hi(q), start=(q == 0), stop=False)
                nc.tensor.matmul(DB[k % 2][:, :], a, lo(q), start=False, stop=False)
                last = nc.tensor.matmul(DB[k % 2][:, :], b, hi(q), start=False, stop=(q == n - 1))
            last.then_inc(s["unit"], 1)

        def x_hi(q):
            return xh[:, q, :]

        def x_lo(q):
            return xl[:, q, :]

        def f_hi(q):
            return fh[:, q, :]

        def f_lo(q):
            return fl[:, q, :]

        def act_tile(act, s, st, j, gain, n):
            scale = 1.0 if isinstance(gain, str) else gain[:, j:j + 1]
            nc.scalar.activation(xh[:, j, :], h[:, j, :], ACT.Copy, scale=scale).then_inc(s["x_hi"], 1)
            act.wait_ge(s["x_hi"], st.up("x_hi"))

        def act_square(act, s, st, src, n):
            if due(n - 1):
                act.wait_ge(s["sq_sum"], n - 1)
            nc.scalar.activation(sq[:, n % 2, :], src, ACT.Square).then_inc(s["sq_done"], 1)
            act.wait_ge(s["sq_done"], st.up("sq_done"))

        def dve_tile(dve, s, st, j, gain, n):
            dve.wait_ge(s["x_hi"], n + 1)
            scale = 1.0 if isinstance(gain, str) else gain[:, j:j + 1]
            nc.vector.scalar_tensor_tensor(xl[:, j, :], h[:, j, :], scale,
                                           xh[:, j, :].bitcast(F32), ALU.mult, ALU.subtract).then_inc(s["x_lo"], 1)
            dve.wait_ge(s["x_lo"], st.up("x_lo"))

        def pe_stat(pe, s, n, first, last, group, mean="mean_d"):
            pe.wait_ge(s["sq_done"], n + 1)
            if first and group:
                pe.wait_ge(s["stat_read"], group)
            nc.tensor.matmul(STAT[:, :], c(mean), sq[:, n % 2, :], start=first, stop=last).then_inc(s["sq_sum"], 1)

        def act_rstd(act, s, st, n):
            act.wait_ge(s["sq_sum"], n)
            nc.scalar.activation(rstd[:, :], STAT[:, :], ACT.Sqrt, bias=c("eps")).then_inc(s["stat_read"], 1)
            act.wait_ge(s["stat_read"], st.up("stat_read"))

        def dve_rstd(dve, s, st, n):
            dve.wait_ge(s["stat_read"], n)
            nc.vector.reciprocal(rstd[:, :], rstd[:, :]).then_inc(s["dve_step"], 1)
            dve.wait_ge(s["dve_step"], st.up("dve_step"))

        def ffn_units(base):
            at_unit, pair = base, 0
            for g, n in enumerate(GROUPS):
                yield g, n, at_unit, pair
                at_unit += 2 * n + DC
                pair += n

        def pe_ffn(pe, s, base, x_ready, ff_before, sq_n, group):
            for g, n, u, pair in ffn_units(base):
                start = 0
                if g == 0:
                    pe_unit(pe, s, 0, u, x_hi, x_lo, chunk_waits=lambda q: ("x_lo", x_ready + q + 1))
                    for k in range(1, 4):
                        pe_unit(pe, s, 0, u + k, x_hi, x_lo)
                    start = 1
                with pe.Fori(start, n // 2) as i:
                    for k in range(4):
                        pe_unit(pe, s, i, u + k, x_hi, x_lo)
                for j in range(DC):
                    k = u + 2 * n + j
                    wait = (lambda q: ("ff_lo", ff_before + pair + q + 1)) if j == 0 else None
                    pe_unit(pe, s, 0, k, f_hi, f_lo, n, wait)
                    if g == len(GROUPS) - 1 and sq_n is not None and j > 0:
                        pe_stat(pe, s, sq_n + j - 1, j == 1, False, group)
            if sq_n is not None:
                pe_stat(pe, s, sq_n + DC - 1, False, True, group)

        def act_ffn(act, s, st, base, ff_before, gain, x_n, sq_n, pair_body, turns):
            for g, n, u, pair in ffn_units(base):
                with act.Fori(0, n // 2) as i, st.turns(i, n // 2, turns):
                    for k in (0, 2):
                        pair_body(act, s, st, i, u + k, i * 2 + k // 2, i * 2 + (ff_before + pair + k // 2), 8 * g)
                for j in range(DC):
                    k = u + 2 * n + j
                    act_split(act, s, st, 0, k + 1)
                    if g == len(GROUPS) - 1:
                        act.wait_ge(s["bank"], k + 1)
                        if gain is not None:
                            act_tile(act, s, st, j, gain, x_n + j)
                        if sq_n is not None:
                            act_square(act, s, st, h[:, j, :], sq_n + j)

        def dve_ffn(dve, s, st, base, ff_before, gain, x_n, factor, pair_body, turns):
            for g, n, u, pair in ffn_units(base):
                with dve.Fori(0, n // 2) as i, st.turns(i, n // 2, turns):
                    for k in (0, 2):
                        pair_body(dve, s, st, i, u + k, i * 2 + k // 2, i * 2 + (ff_before + pair + k // 2), 8 * g)
                for j in range(DC):
                    k = u + 2 * n + j
                    dve_split(dve, s, st, 0, k + 1)
                    dve.wait_ge(s["unit"], k + 1)
                    nc.vector.scalar_tensor_tensor(h[:, j, :], DB[k % 2][:, :], factor, h[:, j, :],
                                                   ALU.mult, ALU.add).then_inc(s["bank"], 1)
                    dve.wait_ge(s["bank"], st.up("bank"))
                    if g == len(GROUPS) - 1 and gain is not None:
                        dve_tile(dve, s, st, j, gain, x_n + j)

        def act_swiglu(act, s, st, i, k, chunk, n, g8):
            act_split(act, s, st, i, k + 1)
            act.wait_ge(s["bank"], i * 4 + (k + 1))
            nc.scalar.activation(sbuf[:, :], gbuf[:, :], ACT.Silu).then_inc(s["silu"], 1)
            act.wait_ge(s["silu"], st.up("silu"))
            act_split(act, s, st, i, k + 2)
            act.wait_ge(s["ff"], n + 1)
            nc.scalar.activation(fh[:, chunk, :], fbuf[:, :], ACT.Copy).then_inc(s["ff_hi"], 1)
            act.wait_ge(s["ff_hi"], st.up("ff_hi"))

        def dve_swiglu(dve, s, st, i, k, chunk, n, g8):
            v = nc.vector
            dve_split(dve, s, st, i, k + 1)
            dve.wait_ge(s["unit"], i * 4 + (k + 1))
            v.tensor_tensor(gbuf[:, :], DB[k % 2][:, :], rstd[:, :], ALU.mult).then_inc(s["bank"], 1)
            dve.wait_ge(s["bank"], st.up("bank"))
            dve_split(dve, s, st, i, k + 2)
            dve.wait_ge(s["unit"], i * 4 + (k + 2))
            v.tensor_tensor(ubuf[:, :], DB[(k + 1) % 2][:, :], rstd[:, :], ALU.mult).then_inc(s["bank"], 1)
            dve.wait_ge(s["bank"], st.up("bank"))
            dve.wait_ge(s["silu"], n + 1)
            v.tensor_tensor(fbuf[:, :], ubuf[:, :], sbuf[:, :], ALU.mult).then_inc(s["ff"], 1)
            dve.wait_ge(s["ff"], st.up("ff"))
            dve.wait_ge(s["ff_hi"], n + 1)
            v.tensor_tensor(fl[:, chunk, :], fbuf[:, :], fh[:, chunk, :].bitcast(F32), ALU.subtract)\
                .then_inc(s["ff_lo"], 1)
            dve.wait_ge(s["ff_lo"], st.up("ff_lo"))

        SWIGLU_ACT = dict(w_hi=4, silu=2, ff_hi=2)
        SWIGLU_DVE = dict(w_lo=4, bank=4, ff=2, ff_lo=2)

        def block1():
            names = COMMON + ["rot_mm", "rot_done", "v_mm", "v_tok", "conv_in", "diag", "tap", "conv_mm",
                              "gate", "p_in", "p_hi", "p_lo", "ple_mm", "ple_ev", "s_mm", "s_ready", "max_ready", "prob", "pt_mm",
                              "pt_ready", "pv_mm", "sink_in", "sink_exp", "o_ready", "o_sum", "o_normed", "o_mm",
                              "mix_hi", "mix_lo", "mean_mm", "y_ready", "xc_ready", "ln_ready", "conv_act",
                              "conv_normed", "e_ready", "sig", "out_done"]
            with ExitStack() as own:
                s = {n: own.enter_context(nc.semaphore(n)) for n in names}
                ids = [v.num for v in s.values()]
                m = Layout(nc, mix_at, sb.end - mix_at)
                small = m("small1", [P, NS1])
                q_t = m("q_t", [P, 4, T])
                k_t = m("k_t", [P, T])
                v_t = m("v_t", [P, T])
                v_tok = m("v_tok", [P, NB, P])
                upad = m("upad", [P, CT, TAPS - 1 + T])
                a = Layout(nc, x_at, 32768)
                sm = a("sm", [P, 2, 2 * P])
                prob = a("prob", [P, 2, 2 * P])
                pt = a("pt", [P, 2, 2 * P])
                o_tok = a("o_tok", [P, 512])
                o_sq = a("o_sq", [P, 512])
                y = a("y", [P, CT, T])
                mx = a("mx", [P, 32])
                negm = a("negm", [P, 32])
                den = a("den", [P, 32])
                es = a("es", [P, 3, H1])
                negsink = a("negsink", [P, H1])
                ss = a("ss", [P, 4])
                diag = a("diag", [P, 8, P])
                f = Layout(nc, f_at, 32768)
                p_t = f("p_t", [P, 2, T])
                p_hi = f("p_hi", [P, 2, T], F32R)
                p_lo = f("p_lo", [P, 2, T], F32R)

                def g(name):
                    o, n = SMALL1[name]
                    return small[:, o:o + n]

                def ple_mm(n):
                    return ("unit", U1_PLE + n // 4 + 1) if n % 4 == 3 else ("ple_mm", n + 1 - n // 4)

                def ple_read(n):
                    return ("bank", U1_PLE + n // 4 + 1) if n % 4 == 3 else ("ple_ev", n + 1 - n // 4)

                taps = g("taps").rearrange("p (c j) -> p c j", c=CT)

                with nc.Fori(0, DEPTH) as layer:
                    with nc.Block() as block:
                        @block.sync
                        def _(sp):
                            sp_weights(sp, s, io["w1"][layer], U1)

                        @block.gpsimd
                        def _(pool):
                            st = Count()
                            pool.wait_ge(s["unit"], U1_IN + 14)
                            for n in range(CT * TAPS):
                                if due(n - 7):
                                    pool.wait_ge(s["tap"], n - 7)
                                nc.gpsimd.tensor_scalar(diag[:, n % 8, :], c("ident"),
                                                        taps[:, n // TAPS, n % TAPS:n % TAPS + 1], None,
                                                        ALU.mult).then_inc(s["diag"], 1)
                                pool.wait_ge(s["diag"], st.up("diag"))

                        @block.tensor
                        def _(pe):
                            st = Count()
                            mm = nc.tensor.matmul
                            for j in range(DC):
                                pe_stat(pe, s, j, j == 0, j == DC - 1, 0)
                            pe_ffn(pe, s, 0, 0, 0, 8, 1)

                            def rotate(n):
                                pe.wait_ge(s["bank"], U1_IN + (1 if n == 0 else n + 2))
                                if due(n - 1):
                                    pe.wait_ge(s["rot_done"], n - 1)
                                mm(BK[n % 2][:, :], c("swap1"), (gbuf, ubuf)[n % 2][:, :], start=True,
                                   stop=True).then_inc(s["rot_mm"], 1)

                            for n in range(14):
                                wait = (lambda q: ("x_lo", 8 + q + 1)) if n == 0 else None
                                pe_unit(pe, s, 0, U1_IN + n, x_hi, x_lo, DC, wait)
                                if n == 1:
                                    rotate(0)
                                if n == 2:
                                    pe.wait_ge(s["bank"], U1_IN + 2)
                                    for b in range(NB):
                                        last = nc.tensor.transpose(BK[2][:, b * P:(b + 1) * P],
                                                                   v_t[:, b * P:(b + 1) * P], c("ident"))
                                    last.then_inc(s["v_mm"], 1)
                                if 3 <= n < 7:
                                    rotate(n - 2)
                            for n in range(DC):
                                u = U1_PLE + n // 4
                                if n % 4 == 0:
                                    pe.wait_ge(s["w_lo"], u + 1)
                                if n == 0:
                                    pe.wait_ge(s["p_lo"], 1)
                                    pe.wait_ge(s["rot_done"], 5)
                                if n >= 2:
                                    pe.wait_ge(s[ple_read(n - 2)[0]], ple_read(n - 2)[1])
                                for q in range(2):
                                    col = (n % 4 * 2 + q) * P
                                    w_h, w_l = wh[u % 2][:, col:col + P], wl[u % 2][:, col:col + P]
                                    mm(BK[n % 2][:, :], w_h, p_hi[:, q, :], start=(q == 0), stop=False)
                                    mm(BK[n % 2][:, :], w_h, p_lo[:, q, :], start=False, stop=False)
                                    last = mm(BK[n % 2][:, :], w_l, p_hi[:, q, :], start=False, stop=(q == 1))
                                last.then_inc(s[ple_mm(n)[0]], 1)
                                if n > 0:
                                    pe_stat(pe, s, 16 + n - 1, n == 1, False, 2)
                            pe_stat(pe, s, 23, False, True, 2)

                            def scores(n):
                                b, hd = divmod(n, H1)
                                rows = slice(hd // 4 * HD, hd // 4 * HD + HD)
                                lo = max(b - 1, 0) * P
                                if due(n - 1):
                                    pe.wait_ge(s["s_ready"], n - 1)
                                if n == 0:
                                    pe.wait_ge(s["rot_done"], 5)
                                    pe.wait_ge(s[ple_read(DC - 1)[0]], ple_read(DC - 1)[1])
                                mm(BK[n % 2][:, 0:(b + 1) * P - lo], q_t[rows, hd % 4, b * P:(b + 1) * P],
                                   k_t[rows, lo:(b + 1) * P], start=True, stop=True).then_inc(s["s_mm"], 1)

                            def tap(n):
                                ct, j = divmod(n, TAPS)
                                if j == 0:
                                    pe.wait_ge(s["conv_in"], ct + 1)
                                    if due(ct):
                                        pe.wait_ge(s["y_ready"], ct)
                                pe.wait_ge(s["diag"], n + 1)
                                mm(BK[4][:, :], diag[:, n % 8, :], upad[:, ct, j:j + T], start=(j == 0),
                                   stop=(j == TAPS - 1)).then_inc(s["tap"], 1)

                            def out_tiles(b):
                                pe.wait_ge(s["o_normed"], b + 1)
                                if due(b):
                                    pe.wait_ge(s["mix_lo"], b)
                                for q in range(4):
                                    last = nc.tensor.transpose(DB[0][:, q * P:(q + 1) * P],
                                                               o_tok[:, q * P:(q + 1) * P], c("ident"))
                                last.then_inc(s["o_mm"], 1)

                            scores(0)
                            for n in range(NB * H1):
                                b, hd = divmod(n, H1)
                                if n + 1 < NB * H1:
                                    scores(n + 1)
                                pe.wait_ge(s["prob"], n + 1)
                                if due(n - 1):
                                    pe.wait_ge(s["pt_ready"], n - 1)
                                keys = 1 if b == 0 else 2
                                for kb in range(keys):
                                    last = nc.tensor.transpose((BK[2], DB[1])[n % 2][:, kb * P:(kb + 1) * P],
                                                               prob[:, n % 2, kb * P:(kb + 1) * P], c("ident"))
                                last.then_inc(s["pt_mm"], 1)
                                for x in range(4 * n, min(4 * n + 4, CT * TAPS)):
                                    tap(x)
                                if hd == 2 and b > 0:
                                    out_tiles(b - 1)
                                pe.wait_ge(s["pt_ready"], n + 1)
                                if n == 0:
                                    pe.wait_ge(s["v_tok"], 1)
                                if hd == 0:
                                    if due(b):
                                        pe.wait_ge(s["o_ready"], b)
                                for kb in range(keys):
                                    last = mm(BK[3][:, hd * HD:(hd + 1) * HD], pt[:, n % 2, kb * P:(kb + 1) * P],
                                              v_tok[:, b - keys + 1 + kb, hd // 4 * HD:hd // 4 * HD + HD],
                                              start=(kb == 0), stop=(kb == keys - 1))
                                last.then_inc(s["pv_mm"], 1)
                            out_tiles(NB - 1)
                            pe.wait_ge(s["stat_read"], 3)
                            for q in range(CT):
                                pe.wait_ge(s["y_ready"], q + 1)
                                mm(STAT[:, :], c("mean_c"), y[:, q, :], start=(q == 0),
                                   stop=(q == CT - 1)).then_inc(s["mean_mm"], 1)
                            for grp in range(2):
                                for q in range(CT):
                                    pe_stat(pe, s, 24 + 4 * grp + q, q == 0, q == CT - 1, 4 + grp, "mean_c")
                            for n in range(DC):
                                pe_unit(pe, s, 0, U1_OUT + n, f_hi, f_lo, DC,
                                        (lambda q: ("mix_lo", NB + max(q - 3, 0))) if n == 0 else None)
                                if n > 0:
                                    pe_stat(pe, s, 32 + n - 1, n == 1, False, 6)
                            pe_stat(pe, s, 39, False, True, 6)
                            pe_ffn(pe, s, U1_FFN2, 16, FC, None, None)
                            for n in range(DC):
                                pe_unit(pe, s, 0, U1_GATE + n, x_hi, x_lo, DC,
                                        (lambda q: ("x_lo", 24 + q + 1)) if n == 0 else None)

                        def finish_a(act, s, st, b):
                            A = nc.scalar.activation
                            act.wait_ge(s["sink_in"], b + 1)
                            A(es[:, 1, :], es[:, 0, :], ACT.Exp).then_inc(s["sink_exp"], 1)
                            act.wait_ge(s["sink_exp"], st.up("sink_exp"))
                            act.wait_ge(s["o_ready"], b + 1)
                            A(o_sq[:, :], o_tok[:, :], ACT.Square, accum_out=ss[:, 0:1]).then_inc(s["act_step"], 1)
                            act.wait_ge(s["act_step"], st.up("act_step"))
                            A(ss[:, 1:2], ss[:, 0:1], ACT.Sqrt, scale=1.0 / 512, bias=c("eps"))\
                                .then_inc(s["o_sum"], 1)
                            act.wait_ge(s["o_sum"], st.up("o_sum"))

                        def finish_b(act, s, st, b):
                            A = nc.scalar.activation
                            act.wait_ge(s["o_mm"], b + 1)
                            A(fh[:, 0:4, b * P:(b + 1) * P], DB[0][:, :].rearrange("p (c t) -> p c t", c=4),
                              ACT.Copy).then_inc(s["mix_hi"], 1)
                            act.wait_ge(s["mix_hi"], st.up("mix_hi"))

                        @block.scalar
                        def _(act):
                            st = Count()
                            A = nc.scalar.activation
                            act.dma_start(small[:, :], io["small1"][layer]).then_inc(s["small_in"], 16)
                            act.wait_ge(s["small_in"], 16)
                            act_split(act, s, st, 0, 0)
                            for j in range(DC):
                                act_tile(act, s, st, j, g("ffn1"), j)
                                act_square(act, s, st, h[:, j, :], j)
                            act_rstd(act, s, st, 8)
                            act_ffn(act, s, st, 0, 0, g("mix"), 8, 8, act_swiglu, SWIGLU_ACT)
                            act_rstd(act, s, st, 16)
                            act.wait_ge(s["unit"], U1_IN)
                            act.dma_start(p_t[:, :, :], io["p1"][layer]).then_inc(s["p_in"], 16)
                            for n in range(14):
                                act_split(act, s, st, 0, U1_IN + n + 1)
                                if n >= 6 and n % 2 == 0:
                                    act.wait_ge(s["bank"], U1_IN + n + 1)
                                    A(sbuf[:, :], v_t[:, :], ACT.Sigmoid).then_inc(s["gate"], 1)
                                    act.wait_ge(s["gate"], st.up("gate"))
                            act.wait_ge(s["p_in"], 16)
                            A(p_hi[:, :, :], p_t[:, :, :], ACT.Copy).then_inc(s["p_hi"], 1)
                            act.wait_ge(s["p_hi"], st.up("p_hi"))
                            for n in range(DC):
                                if n % 4 == 0:
                                    act_split(act, s, st, 0, U1_PLE + n // 4 + 1)
                                act.wait_ge(s[ple_read(n)[0]], ple_read(n)[1])
                                act_square(act, s, st, e_t[:, n, :], 16 + n)
                            act_rstd(act, s, st, 24)

                            for n in range(NB * H1):
                                b, hd = divmod(n, H1)
                                w = P if b == 0 else 2 * P
                                if due(n - 1):
                                    act.wait_ge(s["pt_mm"], n - 1)
                                act.wait_ge(s["max_ready"], n + 1)
                                A(prob[:, n % 2, 0:w], sm[:, n % 2, 0:w], ACT.Exp, scale=HD ** -0.5,
                                  bias=negm[:, n:n + 1], accum_out=den[:, n:n + 1]).then_inc(s["prob"], 1)
                                act.wait_ge(s["prob"], st.up("prob"))
                                if hd == 1 and b > 0:
                                    finish_a(act, s, st, b - 1)
                                if hd == 3 and b > 0:
                                    finish_b(act, s, st, b - 1)
                            finish_a(act, s, st, NB - 1)
                            finish_b(act, s, st, NB - 1)
                            act.wait_ge(s["mean_mm"], CT)
                            A(rstd[:, :], STAT[:, :], ACT.Copy).then_inc(s["stat_read"], 1)
                            act.wait_ge(s["stat_read"], st.up("stat_read"))
                            for q in range(CT):
                                act.wait_ge(s["xc_ready"], q + 1)
                                act_square(act, s, st, y[:, q, :], 24 + q)
                            act_rstd(act, s, st, 28)
                            for q in range(CT):
                                act.wait_ge(s["ln_ready"], q + 1)
                                A(y[:, q, :], y[:, q, :], ACT.Silu, scale=g("ln_g")[:, q:q + 1],
                                  bias=g("ln_b")[:, q:q + 1]).then_inc(s["conv_act"], 1)
                                act.wait_ge(s["conv_act"], st.up("conv_act"))
                                act_square(act, s, st, y[:, q, :], 28 + q)
                            act_rstd(act, s, st, 32)
                            for q in range(CT):
                                act.wait_ge(s["conv_normed"], q + 1)
                                A(fh[:, 4 + q, :], y[:, q, :], ACT.Copy).then_inc(s["mix_hi"], 1)
                                act.wait_ge(s["mix_hi"], st.up("mix_hi"))
                            for n in range(DC):
                                act_split(act, s, st, 0, U1_OUT + n + 1)
                                act.wait_ge(s["bank"], U1_OUT + n + 1)
                                act_tile(act, s, st, n, g("ffn2"), 16 + n)
                                act_square(act, s, st, h[:, n, :], 32 + n)
                            act_rstd(act, s, st, 40)
                            act_ffn(act, s, st, U1_FFN2, FC, "plain", 24, None, act_swiglu, SWIGLU_ACT)
                            for n in range(DC):
                                if n < DC - 1:
                                    act_split(act, s, st, 0, U1_GATE + n + 1)
                                act.wait_ge(s["unit"], U1_GATE + n + 1)
                                if due(n):
                                    act.wait_ge(s["out_done"], n)
                                A(sbuf[:, :], DB[n % 2][:, :], ACT.Sigmoid).then_inc(s["sig"], 1)
                                act.wait_ge(s["sig"], st.up("sig"))

                        @block.vector
                        def _(dve):
                            st = Count()
                            v = nc.vector
                            dve.wait_ge(s["small_in"], 16)
                            dve_split(dve, s, st, 0, 0)
                            for j in range(DC):
                                dve_tile(dve, s, st, j, g("ffn1"), j)
                            dve_rstd(dve, s, st, 1)
                            dve_ffn(dve, s, st, 0, 0, g("mix"), 8, 0.5, dve_swiglu, SWIGLU_DVE)
                            v.memset(upad[:, :, 0:TAPS - 1], 0.0).then_inc(s["dve_step"], 1)
                            dve.wait_ge(s["dve_step"], st.up("dve_step"))

                            def rotate(n, out):
                                buf = (gbuf, ubuf)[n % 2]
                                v.tensor_tensor(fbuf[:, :], buf[:, :], cos[:, :], ALU.mult).then_inc(s["dve_step"], 1)
                                dve.wait_ge(s["dve_step"], st.up("dve_step"))
                                dve.wait_ge(s["rot_mm"], n + 1)
                                v.tensor_tensor(buf[:, :], BK[n % 2][:, :], sin[:, :], ALU.mult)\
                                    .then_inc(s["dve_step"], 1)
                                dve.wait_ge(s["dve_step"], st.up("dve_step"))
                                v.tensor_tensor(out, buf[:, :], fbuf[:, :], ALU.add).then_inc(s["rot_done"], 1)
                                dve.wait_ge(s["rot_done"], st.up("rot_done"))

                            for n in range(14):
                                u = U1_IN + n
                                dve_split(dve, s, st, 0, u + 1)
                                dve.wait_ge(s["unit"], u + 1)
                                if n == 0:
                                    dve_rstd(dve, s, st, 2)
                                if n == 1:
                                    out = v_t
                                elif n < 6:
                                    out = (gbuf, ubuf)[(0, 0, 1, 2, 3, 4)[n] % 2]
                                else:
                                    out = (v_t, ubuf)[n % 2]
                                v.tensor_tensor(out[:, :], DB[u % 2][:, :], rstd[:, :], ALU.mult)\
                                    .then_inc(s["bank"], 1)
                                dve.wait_ge(s["bank"], st.up("bank"))
                                if n == 1:
                                    rotate(0, k_t[:, :])
                                if n == 2:
                                    dve.wait_ge(s["v_mm"], 1)
                                    v.tensor_copy(v_tok[:, :, :], BK[2][:, :].rearrange("p (b f) -> p b f", b=NB))\
                                        .then_inc(s["v_tok"], 1)
                                    dve.wait_ge(s["v_tok"], st.up("v_tok"))
                                if 3 <= n < 7:
                                    rotate(n - 2, q_t[:, n - 3, :])
                                if n >= 6 and n % 2 == 1:
                                    dve.wait_ge(s["gate"], n // 2 - 2)
                                    v.tensor_tensor(upad[:, n // 2 - 3, TAPS - 1:], ubuf[:, :], sbuf[:, :],
                                                    ALU.mult).then_inc(s["conv_in"], 1)
                                    dve.wait_ge(s["conv_in"], st.up("conv_in"))
                            dve.wait_ge(s["p_hi"], 1)
                            v.tensor_tensor(p_lo[:, :, :], p_t[:, :, :], p_hi[:, :, :].bitcast(F32),
                                            ALU.subtract).then_inc(s["p_lo"], 1)
                            dve.wait_ge(s["p_lo"], st.up("p_lo"))
                            for n in range(DC):
                                if n % 4 == 0:
                                    dve_split(dve, s, st, 0, U1_PLE + n // 4 + 1)
                                dve.wait_ge(s[ple_mm(n)[0]], ple_mm(n)[1])
                                v.tensor_copy(e_t[:, n, :], BK[n % 2][:, :]).then_inc(s[ple_read(n)[0]], 1)
                                dve.wait_ge(s[ple_read(n)[0]], st.up(ple_read(n)[0]))
                            dve_rstd(dve, s, st, 3)
                            for n in range(DC):
                                v.scalar_tensor_tensor(e_t[:, n, :], e_t[:, n, :], g("ple")[:, n:n + 1],
                                                       rstd[:, :], ALU.mult, ALU.mult).then_inc(s["dve_step"], 1)
                                dve.wait_ge(s["dve_step"], st.up("dve_step"))

                            v.tensor_scalar(negsink[:, :], g("sinks"), -1.0, None, ALU.mult)\
                                .then_inc(s["dve_step"], 1)
                            dve.wait_ge(s["dve_step"], st.up("dve_step"))

                            def turn_back(n):
                                w = P if n < H1 else 2 * P
                                dve.wait_ge(s["pt_mm"], n + 1)
                                if due(n - 1):
                                    dve.wait_ge(s["pv_mm"], n - 1)
                                v.tensor_copy(pt[:, n % 2, 0:w], (BK[2], DB[1])[n % 2][:, 0:w])\
                                    .then_inc(s["pt_ready"], 1)
                                dve.wait_ge(s["pt_ready"], st.up("pt_ready"))

                            def finish_a(b):
                                cols = slice(b * H1, (b + 1) * H1)
                                v.tensor_tensor(es[:, 0, :], negm[:, cols], g("sinks"), ALU.add)\
                                    .then_inc(s["sink_in"], 1)
                                dve.wait_ge(s["sink_in"], st.up("sink_in"))
                                dve.wait_ge(s["sink_exp"], b + 1)
                                dve.wait_ge(s["prob"], (b + 1) * H1)
                                v.tensor_tensor(den[:, cols], den[:, cols], es[:, 1, :], ALU.add)\
                                    .then_inc(s["dve_step"], 1)
                                dve.wait_ge(s["dve_step"], st.up("dve_step"))
                                v.reciprocal(es[:, 2, :], den[:, cols]).then_inc(s["dve_step"], 1)
                                dve.wait_ge(s["dve_step"], st.up("dve_step"))
                                dve.wait_ge(s["pv_mm"], (b + 1) * H1)
                                if due(b):
                                    dve.wait_ge(s["o_mm"], b)
                                v.tensor_tensor(o_tok[:, :].rearrange("p (h d) -> p h d", h=H1),
                                                BK[3][:, :].rearrange("p (h d) -> p h d", h=H1),
                                                es[:, 2, :].unsqueeze(2).to_broadcast([P, H1, HD]),
                                                ALU.mult).then_inc(s["o_ready"], 1)
                                dve.wait_ge(s["o_ready"], st.up("o_ready"))
                                dve.wait_ge(s["o_sum"], b + 1)
                                v.reciprocal(ss[:, 2:3], ss[:, 1:2]).then_inc(s["dve_step"], 1)
                                dve.wait_ge(s["dve_step"], st.up("dve_step"))
                                v.scalar_tensor_tensor(o_tok[:, :], o_tok[:, :], ss[:, 2:3], g("attn_out"),
                                                       ALU.mult, ALU.mult).then_inc(s["o_normed"], 1)
                                dve.wait_ge(s["o_normed"], st.up("o_normed"))

                            def finish_b(b):
                                dve.wait_ge(s["mix_hi"], b + 1)
                                cols = slice(b * P, (b + 1) * P)
                                v.tensor_tensor(fl[:, 0:4, cols], DB[0][:, :].rearrange("p (c t) -> p c t", c=4),
                                                fh[:, 0:4, cols].bitcast(F32), ALU.subtract).then_inc(s["mix_lo"], 1)
                                dve.wait_ge(s["mix_lo"], st.up("mix_lo"))

                            for n in range(NB * H1):
                                b, hd = divmod(n, H1)
                                w = P if b == 0 else 2 * P
                                dve.wait_ge(s["s_mm"], n + 1)
                                if due(n - 1):
                                    dve.wait_ge(s["prob"], n - 1)
                                v.tensor_tensor_reduce(
                            sm[:, n % 2, 0:w], BK[n % 2][:, 0:w], c("band")[:, 2 * P - w:2 * P], 1.0, NEG,
                            ALU.add, ALU.max, mx[:, n:n + 1]).then_inc(s["s_ready"], 1)
                                dve.wait_ge(s["s_ready"], st.up("s_ready"))
                                v.tensor_scalar(negm[:, n:n + 1], mx[:, n:n + 1], -HD ** -0.5,
                                                negsink[:, hd:hd + 1], ALU.mult, ALU.min).then_inc(s["max_ready"], 1)
                                dve.wait_ge(s["max_ready"], st.up("max_ready"))
                                if n > 0:
                                    turn_back(n - 1)
                                for ct in range(CT):
                                    if n == -(-TAPS * (ct + 1) // 4):
                                        dve.wait_ge(s["tap"], TAPS * (ct + 1))
                                        v.tensor_scalar(y[:, ct, :], BK[4][:, :], g("conv_b")[:, ct:ct + 1],
                                                        None, ALU.add).then_inc(s["y_ready"], 1)
                                        dve.wait_ge(s["y_ready"], st.up("y_ready"))
                                if hd == 1 and b > 0:
                                    finish_a(b - 1)
                                if hd == 3 and b > 0:
                                    finish_b(b - 1)
                            turn_back(NB * H1 - 1)
                            finish_a(NB - 1)
                            finish_b(NB - 1)
                            dve.wait_ge(s["stat_read"], 4)
                            for q in range(CT):
                                v.tensor_tensor(y[:, q, :], y[:, q, :], rstd[:, :], ALU.subtract)\
                                    .then_inc(s["xc_ready"], 1)
                                dve.wait_ge(s["xc_ready"], st.up("xc_ready"))
                            dve_rstd(dve, s, st, 5)
                            for q in range(CT):
                                v.tensor_tensor(y[:, q, :], y[:, q, :], rstd[:, :], ALU.mult)\
                                    .then_inc(s["ln_ready"], 1)
                                dve.wait_ge(s["ln_ready"], st.up("ln_ready"))
                            dve_rstd(dve, s, st, 6)
                            for q in range(CT):
                                v.scalar_tensor_tensor(y[:, q, :], y[:, q, :], g("conv_out")[:, q:q + 1],
                                                       rstd[:, :], ALU.mult, ALU.mult).then_inc(s["conv_normed"], 1)
                                dve.wait_ge(s["conv_normed"], st.up("conv_normed"))
                                dve.wait_ge(s["mix_hi"], NB + q + 1)
                                v.tensor_tensor(fl[:, 4 + q, :], y[:, q, :], fh[:, 4 + q, :].bitcast(F32),
                                                ALU.subtract).then_inc(s["mix_lo"], 1)
                                dve.wait_ge(s["mix_lo"], st.up("mix_lo"))
                            for n in range(DC):
                                u = U1_OUT + n
                                dve_split(dve, s, st, 0, u + 1)
                                dve.wait_ge(s["unit"], u + 1)
                                v.tensor_tensor(h[:, n, :], DB[u % 2][:, :], h[:, n, :], ALU.add)\
                                    .then_inc(s["bank"], 1)
                                dve.wait_ge(s["bank"], st.up("bank"))
                                dve_tile(dve, s, st, n, g("ffn2"), 16 + n)
                            dve_rstd(dve, s, st, 7)
                            dve_ffn(dve, s, st, U1_FFN2, FC, "plain", 24, 0.5, dve_swiglu, SWIGLU_DVE)
                            for n in range(DC):
                                u = U1_GATE + n
                                if n < DC - 1:
                                    dve_split(dve, s, st, 0, u + 1)
                                dve.wait_ge(s["sig"], n + 1)
                                v.tensor_tensor(gbuf[:, :], sbuf[:, :], e_t[:, n, :], ALU.mult).then_inc(s["bank"], 1)
                                dve.wait_ge(s["bank"], st.up("bank"))
                                v.tensor_tensor(h[:, n, :], h[:, n, :], gbuf[:, :], ALU.add)\
                                    .then_inc(s["out_done"], 1)
                                dve.wait_ge(s["out_done"], st.up("out_done"))
                    nc.gpsimd.sem_clear(range(min(ids), max(ids) + 1))
                    nc.all_engine_barrier()

        def block2():
            names = COMMON + ["rows_ready", "tap0", "conv_done", "z_ready", "post_mm", "post_done", "p_in", "p_hi",
                              "p_lo", "ple_mm", "ple_ev", "sig", "out_done", "gate_conv",
                              "l2_mm", "l2_root", "l2_done", "sp_a", "g_rows", "g_exp", "rows_mm", "tok_ready",
                              "tok_exp", "last_mm", "last_exp", "pre_mm", "pre_exp", "kb_ready", "qg_ready",
                              "tile_ready", "z_tok", "dec_mm", "dec", "kq_mm", "kq_ready", "b_ready", "t_ready",
                              "tt_mm", "u_mm", "u_ready", "v_mm", "inv_ready", "tri_ready", "l2_sq", "uw_mm", "uw_ready", "vn_mm",
                              "vn_ready", "os_mm", "s_state", "o_copy", "o_sq", "o_red", "o_root", "gdn_done",
                              "z_mm", "z_abs", "z_ln", "z_sp", "e_mm", "e_exp", "sbo_mm", "sb_done",
                              "w1_in", "dup_mm", "dup_ready", "hid_mm", "hid", "cmp_mm", "cmp_kv", "cs_mm", "cs_sub",
                              "cs_exp", "ct_mm", "ct_ready", "co_mm", "s_mm", "s_ready", "max_ready", "prob",
                              "pt_mm", "pt_ready", "pv_mm", "nsa_done", "hn_sq", "hn_red", "hn_root", "hn_done",
                              "o_mm", "mix_hi", "mix_lo", "e_ready"]
            with ExitStack() as own:
                s = {n: own.enter_context(nc.semaphore(n)) for n in names}
                ids = [v.num for v in s.values()]
                m = Layout(nc, mix_at, sb.end - mix_at)
                small = m("small2", [P, NS2])
                p2 = Layout(nc, m.at, 14336)
                z_t = m("z_t", [P, 3, T])
                sq_t = m("sq_t", [P, 2, T])
                sk_t = m("sk_t", [P, 2, T])
                tok = m("tok", [P, 4, NB, P])
                rows_t = m("rows_t", [P, T])
                rows_k = m("rows_k", [P, NB, P])
                o_all = Layout(nc, e_at, 16384)("o_all", [P, NB, D])
                cbuf = m("cbuf", [P, 2, T + 3])
                ybuf = m("ybuf", [P, T])
                f = Layout(nc, f_at, 32768)
                qkv = f("qkv", [P, 9, T])
                roped = f("roped", [P, 6, T])
                vc_t = f("vc_t", [P, T])
                p_t = p2("p_t2", [P, 2, T])
                p_hi = p2("p_hi2", [P, 2, T], F32R)
                p_lo = p2("p_lo2", [P, 2, T], F32R)

                def g(name):
                    o, n = SMALL2[name]
                    return small[:, o:o + n]

                gtaps = g("conv").rearrange("p (c j) -> p c j", c=9)
                ftaps = g("fconv").rearrange("p (c j) -> p c j", j=3)
                posted = [n for n, (kind, _) in enumerate(IN2) if kind in ("rope", "tok")]

                def ple_mm(n):
                    return ("unit", U2_PLE + n // 4 + 1) if n % 4 == 3 else ("ple_mm", n + 1 - n // 4)

                def ple_read(n):
                    return ("bank", U2_PLE + n // 4 + 1) if n % 4 == 3 else ("ple_ev", n + 1 - n // 4)

                def act_conv_pair(act, s, st, i, k, chunk, n, g8):
                    w = chunk * 2 + 2 * g8
                    act_split(act, s, st, i, k + 1)
                    act.wait_ge(s["bank"], i * 4 + (k + 1))
                    nc.scalar.activation(ybuf[:, :], cbuf[:, 0, 3:], ACT.Copy, scale=ftaps[:, w, 2:3])\
                        .then_inc(s["tap0"], 1)
                    act.wait_ge(s["tap0"], st.up("tap0"))
                    act_split(act, s, st, i, k + 2)
                    act.wait_ge(s["gate_conv"], n + 1)
                    nc.scalar.activation(sbuf[:, :], ybuf[:, :], ACT.Silu).then_inc(s["silu"], 1)
                    act.wait_ge(s["silu"], st.up("silu"))
                    act.wait_ge(s["bank"], i * 4 + (k + 2))
                    nc.scalar.activation(ubuf[:, :], cbuf[:, 1, 3:], ACT.Copy, scale=ftaps[:, w + 1, 2:3])\
                        .then_inc(s["tap0"], 1)
                    act.wait_ge(s["tap0"], st.up("tap0"))
                    act.wait_ge(s["ff"], n + 1)
                    nc.scalar.activation(fh[:, chunk, :], fbuf[:, :], ACT.Copy).then_inc(s["ff_hi"], 1)
                    act.wait_ge(s["ff_hi"], st.up("ff_hi"))

                def dve_conv_pair(dve, s, st, i, k, chunk, n, g8):
                    v = nc.vector
                    w = chunk * 2 + 2 * g8
                    dve_split(dve, s, st, i, k + 1)
                    dve.wait_ge(s["unit"], i * 4 + (k + 1))
                    v.tensor_tensor(cbuf[:, 0, 3:], DB[k % 2][:, :], rstd[:, :], ALU.mult).then_inc(s["bank"], 1)
                    dve.wait_ge(s["bank"], st.up("bank"))
                    dve.wait_ge(s["tap0"], n * 2 + 10)
                    v.scalar_tensor_tensor(ybuf[:, :], cbuf[:, 0, 2:2 + T], ftaps[:, w, 1:2], ybuf[:, :],
                                           ALU.mult, ALU.add).then_inc(s["dve_step"], 1)
                    dve.wait_ge(s["dve_step"], st.up("dve_step"))
                    v.scalar_tensor_tensor(ybuf[:, :], cbuf[:, 0, 1:1 + T], ftaps[:, w, 0:1], ybuf[:, :],
                                           ALU.mult, ALU.add).then_inc(s["gate_conv"], 1)
                    dve.wait_ge(s["gate_conv"], st.up("gate_conv"))
                    dve_split(dve, s, st, i, k + 2)
                    dve.wait_ge(s["unit"], i * 4 + (k + 2))
                    v.tensor_tensor(cbuf[:, 1, 3:], DB[(k + 1) % 2][:, :], rstd[:, :], ALU.mult)\
                        .then_inc(s["bank"], 1)
                    dve.wait_ge(s["bank"], st.up("bank"))
                    dve.wait_ge(s["tap0"], n * 2 + 11)
                    v.scalar_tensor_tensor(ubuf[:, :], cbuf[:, 1, 2:2 + T], ftaps[:, w + 1, 1:2], ubuf[:, :],
                                           ALU.mult, ALU.add).then_inc(s["dve_step"], 1)
                    dve.wait_ge(s["dve_step"], st.up("dve_step"))
                    v.scalar_tensor_tensor(ubuf[:, :], cbuf[:, 1, 1:1 + T], ftaps[:, w + 1, 0:1], ubuf[:, :],
                                           ALU.mult, ALU.add).then_inc(s["dve_step"], 1)
                    dve.wait_ge(s["dve_step"], st.up("dve_step"))
                    dve.wait_ge(s["silu"], n + 1)
                    v.tensor_tensor(fbuf[:, :], ubuf[:, :], sbuf[:, :], ALU.mult).then_inc(s["ff"], 1)
                    dve.wait_ge(s["ff"], st.up("ff"))
                    dve.wait_ge(s["ff_hi"], n + 1)
                    v.tensor_tensor(fl[:, chunk, :], fbuf[:, :], fh[:, chunk, :].bitcast(F32), ALU.subtract)\
                        .then_inc(s["ff_lo"], 1)
                    dve.wait_ge(s["ff_lo"], st.up("ff_lo"))

                CONV_ACT = dict(w_hi=4, silu=2, ff_hi=2, tap0=4)
                CONV_DVE = dict(w_lo=4, bank=4, gate_conv=2, ff=2, ff_lo=2, dve_step=6)

                a = Layout(nc, x_at, 32768)
                hd2 = lambda name, shape: [a(f"{name}{n}", shape) for n in range(2)]
                dec, a_t, att, tri, tri_t, mid, low = (hd2(n, [P, NB, P]) for n in
                                                       ("dec", "a_t", "att", "tri", "tri_t", "mid", "low"))
                k_be = a("k_be", [P, NB, P])
                k_gl = a("k_gl", [P, NB, P])
                b2_ = Layout(nc, gbuf_at, 12288)
                v_b = b2_("v_b", [P, NB, P])
                kb_t = b2_("kb_t", [P, T])
                qg_t = b2_("qg_t", [P, T])
                z_k = b2_("z_k", [P, NB, P])
                e_g = b2_("e_g", [P, T])
                u_k, w_t = low[0], low[1]
                o_g = dec[0]
                v_new = mid[0]
                state = m("state", [P, P])
                tiny = m("tiny", [P, 256])
                eg, egl, bet, beg = (tiny[:, n * 24:(n + 1) * 24].rearrange("p (b h) -> p b h", b=NB) for n in range(4))
                last = tiny[:, 96:108].rearrange("p (t b) -> p t b", t=3)
                osum = tiny[:, 112:120]
                oroot = tiny[:, 120:128]
                gate_w = tiny[:, 128:200].rearrange("p (b c) -> p b c", b=NB)
                g6 = rows_t[0:6, :]
                ALL = slice(0, P)

                def by_head(ap):
                    return ap.rearrange("p b (h d) -> p b h d", d=HD)

                def col_bc(ap, shape):
                    return ap.unsqueeze(len(shape) - 1).to_broadcast(shape)

                def pe_gdn(pe, s, st):
                    mm, tr = nc.tensor.matmul, nc.tensor.transpose
                    for n in range(6):
                        pe.wait_ge(s["l2_sq"], n + 1)
                        if due(n - 1):
                            pe.wait_ge(s["l2_root"], n - 1)
                        mm(BK[n % 2][:, :], c("head_sum"), sq[:, n % 2, :], start=True, stop=True)\
                            .then_inc(s["l2_mm"], 1)
                    pe.wait_ge(s["g_rows"], 1)
                    for b in range(NB):
                        tr(BK[2][:, b * P:(b + 1) * P], rows_t[:, b * P:(b + 1) * P], c("ident"))
                    for t in range(GT):
                        ins = mm(BK[3][:, 4 * t:4 * t + 4], c("pick2")[0:6, t * P:(t + 1) * P], g6[:, P - 1::P],
                                 start=True, stop=True)
                    ins.then_inc(s["rows_mm"], 1)
                    pe.wait_ge(s["l2_done"], 6)
                    pe.wait_ge(s["last_exp"], 1)
                    pe.wait_ge(s["kb_ready"], 1)
                    for t in range(GT):
                        if due(t):
                            pe.wait_ge(s["gdn_done"], t)
                        for b in range(NB):
                            blk = slice(b * P, (b + 1) * P)
                            tr(BK[0][:, blk], qkv[:, 3 + t, blk], c("ident"))
                            tr(BK[1][:, blk], qkv[:, 6 + t, blk], c("ident"))
                            tr(BK[2][:, blk], z_t[:, t, blk], c("ident"))
                        mm(DB[0][:, :], c("pick2")[32:38, t * P:(t + 1) * P], rows_t[32:38, :], start=True, stop=True)
                        mm(DB[1][:, :], c("pick2")[0:6, t * P:(t + 1) * P], g6, start=True, stop=True)\
                            .then_inc(s["pre_mm"], 1)
                        for hd in range(2):
                            bank = (STAT, BK[4])[hd]
                            pick = c("pick")[0:6, (2 * t + hd) * P:(2 * t + hd + 1) * P]
                            mm(bank[:, :], pick, g6, start=True, stop=False)
                            for b in range(NB):
                                blk = slice(b * P, (b + 1) * P)
                                mm(bank[:, blk], ybuf[0:6, blk], pick, start=False, stop=False)
                            mm(bank[:, :], c("ident"), c("seen"), start=False, stop=True).then_inc(s["dec_mm"], 1)
                        pe.wait_ge(s["tile_ready"], t + 1)
                        pe.wait_ge(s["pre_exp"], 2 * t + 2)
                        for hd in range(2):
                            r = slice(hd * HD, hd * HD + HD)
                            for b in range(NB):
                                blk = slice(b * P, (b + 1) * P)
                                mm(BK[2 * hd][:, blk], qkv[r, 3 + t, blk], kb_t[r, blk], start=True, stop=True)
                            for b in range(NB):
                                blk = slice(b * P, (b + 1) * P)
                                ins = mm(BK[2 * hd + 1][:, blk], qkv[r, 3 + t, blk], qkv[r, t, blk], start=True,
                                         stop=True)
                            ins.then_inc(s["kq_mm"], 1)
                        for hd in range(2):
                            pe.wait_ge(s["t_ready"], 2 * t + hd + 1)
                            for b in range(NB):
                                ins = tr(BK[2 * hd][:, b * P:(b + 1) * P], tri_t[hd][:, b, :], c("ident"))
                            ins.then_inc(s["tt_mm"], 1)
                        for lv in range(1, LEVELS + 1):
                            for hd in range(2):
                                n = (t * LEVELS + lv - 1) * 2 + hd
                                pe.wait_ge(s["b_ready"], (t * (LEVELS + 1) + lv) * 2 + hd + 1)
                                if lv == 1:
                                    pe.wait_ge(s["tri_ready"], 2 * t + hd + 1)
                                else:
                                    pe.wait_ge(s["inv_ready"], n - 1)
                                for b in range(NB):
                                    ins = mm(DB[hd][:, b * P:(b + 1) * P], low[hd][:, b, :], tri[hd][:, b, :],
                                             start=True, stop=True)
                                ins.then_inc(s["u_mm"], 1)
                            for hd in range(2):
                                n = (t * LEVELS + lv - 1) * 2 + hd
                                pe.wait_ge(s["u_ready"], n + 1)
                                if lv < LEVELS:
                                    for b in range(NB):
                                        mm(BK[2 * hd][:, b * P:(b + 1) * P], tri_t[hd][:, b, :], mid[hd][:, b, :],
                                           start=True, stop=True)
                                for b in range(NB):
                                    ins = mm(BK[2 * hd + 1][:, b * P:(b + 1) * P], mid[hd][:, b, :],
                                             tri_t[hd][:, b, :], start=True, stop=True)
                                ins.then_inc(s["v_mm"], 1)
                        pe.wait_ge(s["inv_ready"], (t + 1) * LEVELS * 2)
                        for hd in range(2):
                            cols = slice(hd * HD, hd * HD + HD)
                            for b in range(NB):
                                blk = slice(b * P, (b + 1) * P)
                                mm(DB[0][:, b * P + hd * HD:b * P + hd * HD + HD], tri_t[hd][:, b, :],
                                   v_b[:, b, cols], start=True, stop=True)
                                ins = mm(DB[1][cols, blk], k_be[:, b, cols], tri_t[hd][:, b, :], start=True,
                                         stop=True)
                        ins.then_inc(s["uw_mm"], 1)
                        pe.wait_ge(s["uw_ready"], t + 1)
                        for b in range(NB):
                            blk = slice(b * P, (b + 1) * P)
                            if b:
                                pe.wait_ge(s["s_state"], 2 * (3 * t + b))
                                mm(BK[0][:, 0:P], w_t[:, blk], state[:, :], start=True, stop=True)\
                                    .then_inc(s["vn_mm"], 1)
                                pe.wait_ge(s["vn_ready"], 3 * t + b)
                            new = v_new if b else u_k
                            if b < NB - 1:
                                mm(BK[2][:, 0:P], k_gl[:, b, :], new[:, b, :], start=True, stop=True)
                            if b:
                                mm(BK[1][:, blk], qg_t[:, blk], state[:, :], start=True, stop=False)
                            for hd in range(2):
                                r = slice(hd * HD, hd * HD + HD)
                                o = BK[1][:, b * P + hd * HD:b * P + hd * HD + HD]
                                ins = mm(o, att[hd][:, b, :], new[:, b, r], start=(b == 0),
                                         stop=(b == 0 or hd == 1))
                            ins.then_inc(s["os_mm"], 1)

                def blk_of(b):
                    return slice(b * P, (b + 1) * P)

                def act_gdn(act, s, st):
                    A = nc.scalar.activation
                    A(rows_t[32:38, :], rows_t[32:38, :], ACT.Sigmoid).then_inc(s["act_step"], 1)
                    act.wait_ge(s["act_step"], st.up("act_step"))
                    A(rows_t[64:82, :], rows_t[64:82, :], ACT.Sigmoid).then_inc(s["act_step"], 1)
                    act.wait_ge(s["act_step"], st.up("act_step"))
                    act.wait_ge(s["sp_a"], 1)
                    A(ybuf[0:6, :], ybuf[0:6, :], ACT.Exp).then_inc(s["act_step"], 1)
                    act.wait_ge(s["act_step"], st.up("act_step"))
                    A(tiny[0:6, 110:111], g("a_log")[0:6, :], ACT.Exp).then_inc(s["act_step"], 1)
                    act.wait_ge(s["act_step"], st.up("act_step"))
                    A(ybuf[0:6, :], ybuf[0:6, :], ACT.Ln, bias=1.0).then_inc(s["g_exp"], 1)
                    act.wait_ge(s["g_exp"], st.up("g_exp"))
                    for n in range(7):
                        if n < 6:
                            if due(n - 1):
                                act.wait_ge(s["l2_mm"], n - 1)
                            A(sq[:, n % 2, :], qkv[:, n, :], ACT.Square).then_inc(s["l2_sq"], 1)
                            act.wait_ge(s["l2_sq"], st.up("l2_sq"))
                        if n > 0:
                            act.wait_ge(s["l2_mm"], n)
                            if due(n - 2):
                                act.wait_ge(s["l2_done"], n - 2)
                            A((gbuf, ubuf)[(n - 1) % 2][:, :], BK[(n - 1) % 2][:, :], ACT.Sqrt,
                              bias=c("eps")).then_inc(s["l2_root"], 1)
                            act.wait_ge(s["l2_root"], st.up("l2_root"))
                    act.wait_ge(s["tok_ready"], 1)
                    A(eg, rows_k[:, :, 0:6], ACT.Exp).then_inc(s["act_step"], 1)
                    act.wait_ge(s["act_step"], st.up("act_step"))
                    A(egl, rows_k[:, :, 96:102], ACT.Exp).then_inc(s["tok_exp"], 1)
                    act.wait_ge(s["tok_exp"], st.up("tok_exp"))
                    A(last, BK[3][:, 0:12].rearrange("p (t b) -> p t b", t=3), ACT.Exp).then_inc(s["last_exp"], 1)
                    act.wait_ge(s["last_exp"], st.up("last_exp"))
                    for t in range(GT):
                        act.wait_ge(s["pre_mm"], t + 1)
                        A(e_g[:, :], DB[1][:, :], ACT.Exp).then_inc(s["pre_exp"], 1)
                        act.wait_ge(s["pre_exp"], st.up("pre_exp"))
                        A(z_k[:, :, :], BK[2][:, :].rearrange("p (b f) -> p b f", b=NB), ACT.Silu)\
                            .then_inc(s["pre_exp"], 1)
                        act.wait_ge(s["pre_exp"], st.up("pre_exp"))
                        for hd in range(2):
                            act.wait_ge(s["dec_mm"], 2 * t + hd + 1)
                            A(dec[hd][:, :, :], (STAT, BK[4])[hd][:, :].rearrange("p (b f) -> p b f", b=NB),
                              ACT.Exp).then_inc(s["dec"], 1)
                            act.wait_ge(s["dec"], st.up("dec"))
                        for hd in range(2):
                            act.wait_ge(s["tt_mm"], 2 * t + hd + 1)
                            A(tri[hd][:, :, :], BK[2 * hd][:, :].rearrange("p (b f) -> p b f", b=NB),
                              ACT.Copy).then_inc(s["tri_ready"], 1)
                            act.wait_ge(s["tri_ready"], st.up("tri_ready"))
                        for lv in range(1, LEVELS + 1):
                            for hd in range(2):
                                n = (t * LEVELS + lv - 1) * 2 + hd
                                act.wait_ge(s["u_mm"], n + 1)
                                if lv > 1:
                                    act.wait_ge(s["v_mm"], n - 1)
                                A(mid[hd][:, :, :], DB[hd][:, :].rearrange("p (b f) -> p b f", b=NB),
                                  ACT.Copy).then_inc(s["u_ready"], 1)
                                act.wait_ge(s["u_ready"], st.up("u_ready"))
                        act.wait_ge(s["o_copy"], t + 1)
                        A(dec[1][:, :, :], o_g[:, :, :], ACT.Square).then_inc(s["o_sq"], 1)
                        act.wait_ge(s["o_sq"], st.up("o_sq"))
                        act.wait_ge(s["o_red"], t + 1)
                        A(oroot, osum, ACT.Sqrt, scale=1.0 / HD, bias=c("eps")).then_inc(s["o_root"], 1)
                        act.wait_ge(s["o_root"], st.up("o_root"))

                def pool_gdn(pool, s, st):
                    for t in range(GT):
                        for lv in range(LEVELS + 1):
                            for hd in range(2):
                                if lv == 0:
                                    pool.wait_ge(s["kq_ready"], 2 * t + hd + 1)
                                elif lv == 1:
                                    pool.wait_ge(s["t_ready"], 2 * t + hd + 1)
                                else:
                                    pool.wait_ge(s["u_mm"], (t * LEVELS + lv - 2) * 2 + hd + 1)
                                nc.gpsimd.tensor_tensor(
                            low[hd][:, :, :], a_t[hd][:, :, :],
                            c(f"level{lv}").unsqueeze(1).to_broadcast([P, NB, P]), ALU.mult).then_inc(s["b_ready"], 1)
                                pool.wait_ge(s["b_ready"], st.up("b_ready"))

                def dve_gdn(dve, s, st):
                    v = nc.vector
                    v.memset(state[:, :], 0.0).then_inc(s["dve_step"], 1)
                    dve.wait_ge(s["dve_step"], st.up("dve_step"))
                    v.tensor_scalar(fbuf[0:6, :], rows_t[0:6, :], g("dt")[0:6, :], None, ALU.add)\
                        .then_inc(s["dve_step"], 1)
                    dve.wait_ge(s["dve_step"], st.up("dve_step"))
                    v.scalar_tensor_tensor(ybuf[0:6, :], fbuf[0:6, :], -1.0, fbuf[0:6, :], ALU.mult, ALU.min)\
                        .then_inc(s["sp_a"], 1)
                    dve.wait_ge(s["sp_a"], st.up("sp_a"))
                    dve.wait_ge(s["g_exp"], 1)
                    v.scalar_tensor_tensor(fbuf[0:6, :], fbuf[0:6, :], 0.0, ybuf[0:6, :], ALU.max, ALU.add)\
                        .then_inc(s["dve_step"], 1)
                    dve.wait_ge(s["dve_step"], st.up("dve_step"))
                    v.tensor_scalar(fbuf[0:6, :], fbuf[0:6, :], tiny[0:6, 110:111], -1.0, ALU.mult, ALU.mult)\
                        .then_inc(s["dve_step"], 1)
                    dve.wait_ge(s["dve_step"], st.up("dve_step"))
                    v.memset(sbuf[0:6, :], 1.0).then_inc(s["dve_step"], 1)
                    dve.wait_ge(s["dve_step"], st.up("dve_step"))
                    for b in range(NB):
                        v.tensor_tensor_scan(g6[:, blk_of(b)], sbuf[0:6, blk_of(b)], fbuf[0:6, blk_of(b)],
                                             0.0, ALU.mult, ALU.add).then_inc(s["dve_step"], 1)
                        dve.wait_ge(s["dve_step"], st.up("dve_step"))
                    v.tensor_scalar(ybuf[0:6, :], g6, -1.0, None, ALU.mult).then_inc(s["dve_step"], 1)
                    dve.wait_ge(s["dve_step"], st.up("dve_step"))
                    gb = g6.rearrange("p (b t) -> p b t", b=NB)
                    v.tensor_tensor(rows_t[96:102, :].rearrange("p (b t) -> p b t", b=NB),
                                    gb[:, :, P - 1:P].to_broadcast([6, NB, P]), gb, ALU.subtract)\
                        .then_inc(s["g_rows"], 1)
                    dve.wait_ge(s["g_rows"], st.up("g_rows"))
                    for n in range(6):
                        dve.wait_ge(s["l2_root"], n + 1)
                        buf = (gbuf, ubuf)[n % 2]
                        v.reciprocal(buf[:, :], buf[:, :]).then_inc(s["dve_step"], 1)
                        dve.wait_ge(s["dve_step"], st.up("dve_step"))
                        v.scalar_tensor_tensor(qkv[:, n, :], buf[:, :], HD ** -0.5 if n < 3 else 1.0,
                                               qkv[:, n, :], ALU.mult, ALU.mult).then_inc(s["l2_done"], 1)
                        dve.wait_ge(s["l2_done"], st.up("l2_done"))
                    dve.wait_ge(s["rows_mm"], 1)
                    v.tensor_copy(rows_k[:, :, :], BK[2][:, :].rearrange("p (b f) -> p b f", b=NB))\
                        .then_inc(s["tok_ready"], 1)
                    dve.wait_ge(s["tok_ready"], st.up("tok_ready"))
                    v.tensor_copy(bet, rows_k[:, :, 32:38]).then_inc(s["dve_step"], 1)
                    dve.wait_ge(s["dve_step"], st.up("dve_step"))
                    v.tensor_copy(gate_w, rows_k[:, :, 64:82]).then_inc(s["dve_step"], 1)
                    dve.wait_ge(s["dve_step"], st.up("dve_step"))
                    dve.wait_ge(s["tok_exp"], 1)
                    v.tensor_tensor(beg, bet, eg, ALU.mult).then_inc(s["kb_ready"], 1)
                    dve.wait_ge(s["kb_ready"], st.up("kb_ready"))
                    for t in range(GT):
                        sh = [P, NB, 2, HD]
                        h2 = slice(2 * t, 2 * t + 2)
                        dve.wait_ge(s["pre_mm"], t + 1)
                        kps = BK[0][:, :].rearrange("p (b h d) -> p b h d", b=NB, h=2)
                        vps = BK[1][:, :].rearrange("p (b h d) -> p b h d", b=NB, h=2)
                        v.tensor_tensor(by_head(k_be[:, :, :]), kps, col_bc(beg[:, :, h2], sh), ALU.mult)\
                            .then_inc(s["dve_step"], 1)
                        dve.wait_ge(s["dve_step"], st.up("dve_step"))
                        v.tensor_tensor(by_head(k_gl[:, :, :]), kps, col_bc(egl[:, :, h2], sh), ALU.mult)\
                            .then_inc(s["dve_step"], 1)
                        dve.wait_ge(s["dve_step"], st.up("dve_step"))
                        v.tensor_tensor(by_head(v_b[:, :, :]), vps, col_bc(bet[:, :, h2], sh), ALU.mult)\
                            .then_inc(s["dve_step"], 1)
                        dve.wait_ge(s["dve_step"], st.up("dve_step"))
                        v.tensor_tensor(kb_t[:, :], DB[0][:, :], qkv[:, 3 + t, :], ALU.mult)\
                            .then_inc(s["dve_step"], 1)
                        dve.wait_ge(s["dve_step"], st.up("dve_step"))
                        dve.wait_ge(s["pre_exp"], 2 * t + 1)
                        v.tensor_tensor(qg_t[:, :], e_g[:, :], qkv[:, t, :], ALU.mult).then_inc(s["tile_ready"], 1)
                        dve.wait_ge(s["tile_ready"], st.up("tile_ready"))
                        for hd in range(2):
                            dve.wait_ge(s["kq_mm"], 2 * t + hd + 1)
                            dve.wait_ge(s["dec"], 2 * t + hd + 1)
                            view = lambda x: x[:, :].rearrange("p (b f) -> p b f", b=NB)
                            v.tensor_tensor(a_t[hd][:, :, :], view(BK[2 * hd]), dec[hd][:, :, :], ALU.mult)\
                                .then_inc(s["dve_step"], 1)
                            dve.wait_ge(s["dve_step"], st.up("dve_step"))
                            v.tensor_tensor(att[hd][:, :, :], view(BK[2 * hd + 1]), dec[hd][:, :, :],
                                            ALU.mult).then_inc(s["kq_ready"], 1)
                            dve.wait_ge(s["kq_ready"], st.up("kq_ready"))
                        for hd in range(2):
                            dve.wait_ge(s["b_ready"], t * (LEVELS + 1) * 2 + hd + 1)
                            v.tensor_tensor(tri_t[hd][:, :, :],
                                            c("ident").unsqueeze(1).to_broadcast([P, NB, P]),
                                            low[hd][:, :, :], ALU.subtract).then_inc(s["t_ready"], 1)
                            dve.wait_ge(s["t_ready"], st.up("t_ready"))
                        for lv in range(1, LEVELS + 1):
                            for hd in range(2):
                                n = (t * LEVELS + lv - 1) * 2 + hd
                                dve.wait_ge(s["v_mm"], n + 1)
                                if lv < LEVELS:
                                    v.tensor_tensor(tri[hd][:, :, :], tri[hd][:, :, :], view(BK[2 * hd]),
                                                    ALU.subtract).then_inc(s["dve_step"], 1)
                                    dve.wait_ge(s["dve_step"], st.up("dve_step"))
                                v.tensor_tensor(tri_t[hd][:, :, :], tri_t[hd][:, :, :],
                                                view(BK[2 * hd + 1]), ALU.subtract).then_inc(s["inv_ready"], 1)
                                dve.wait_ge(s["inv_ready"], st.up("inv_ready"))
                        dve.wait_ge(s["uw_mm"], t + 1)
                        v.tensor_copy(u_k[:, :, :], view(DB[0])).then_inc(s["dve_step"], 1)
                        dve.wait_ge(s["dve_step"], st.up("dve_step"))
                        v.tensor_copy(w_flat, DB[1][:, :]).then_inc(s["uw_ready"], 1)
                        dve.wait_ge(s["uw_ready"], st.up("uw_ready"))
                        for b in range(NB):
                            if b:
                                dve.wait_ge(s["vn_mm"], 3 * t + b)
                                v.tensor_tensor(v_new[:, b, :], u_k[:, b, :], BK[0][:, 0:P], ALU.subtract)\
                                    .then_inc(s["vn_ready"], 1)
                                dve.wait_ge(s["vn_ready"], st.up("vn_ready"))
                            dve.wait_ge(s["os_mm"], 4 * t + b + 1)
                            for hd in range(2) if b < NB - 1 else ():
                                r = slice(hd * HD, hd * HD + HD)
                                if b == 0:
                                    v.tensor_copy(state[r, r], BK[2][r, r]).then_inc(s["s_state"], 1)
                                    dve.wait_ge(s["s_state"], st.up("s_state"))
                                else:
                                    v.scalar_tensor_tensor(state[r, r], state[r, r], last[r, t, b:b + 1],
                                                           BK[2][r, r], ALU.mult, ALU.add).then_inc(s["s_state"], 1)
                                    dve.wait_ge(s["s_state"], st.up("s_state"))
                        v.tensor_copy(o_g[:, :, :], view(BK[1])).then_inc(s["o_copy"], 1)
                        dve.wait_ge(s["o_copy"], st.up("o_copy"))
                        dve.wait_ge(s["o_sq"], t + 1)
                        o3 = o_g[:, :, :].rearrange("p b (h d) -> p (b h) d", d=HD)
                        v.tensor_reduce(osum, dec[1][:, :, :].rearrange("p b (h d) -> p (b h) d", d=HD), AX_X,
                                        ALU.add).then_inc(s["o_red"], 1)
                        dve.wait_ge(s["o_red"], st.up("o_red"))
                        dve.wait_ge(s["o_root"], t + 1)
                        v.reciprocal(oroot, oroot).then_inc(s["dve_step"], 1)
                        dve.wait_ge(s["dve_step"], st.up("dve_step"))
                        v.tensor_tensor(o3, o3, col_bc(oroot, [P, 8, HD]), ALU.mult).then_inc(s["dve_step"], 1)
                        dve.wait_ge(s["dve_step"], st.up("dve_step"))
                        v.tensor_tensor(o3, o3, g("gdn_norm").unsqueeze(1).to_broadcast([P, 8, HD]), ALU.mult)\
                            .then_inc(s["dve_step"], 1)
                        dve.wait_ge(s["dve_step"], st.up("dve_step"))
                        v.tensor_tensor(o_all[:, :, t * P:(t + 1) * P], o_g[:, :, :], z_k[:, :, :], ALU.mult)\
                            .then_inc(s["gdn_done"], 1)
                        dve.wait_ge(s["gdn_done"], st.up("gdn_done"))

                w_flat = w_t[:, :, :].rearrange("p b f -> p (b f)")
                w_t = w_flat

                cl = Layout(nc, x_at, 32768)
                sp_b = [cl(f"sp{n}", [P, 1280]) for n in range(2)]
                a_b = [cl(f"stick{n}", [P, 1280]) for n in range(2)]
                az = cl("az", [P, 2, T])
                w1k = cl("w1k", [P, 16, P])
                w1v = Layout(nc, gbuf_at, 12288)("w1v", [P, 16, P])
                OFF = [0, 512, 896, 1152, 1280]

                def pe_sb(pe, s, st):
                    mm = nc.tensor.matmul

                    def logits(bank, hd, kb, more):
                        r = slice(hd % 2 * HD, hd % 2 * HD + HD)
                        n = T - kb * P
                        mm(bank[:, 0:n], sk_t[r, hd // 2, blk_of(kb)], sq_t[r, hd // 2, kb * P:], start=True,
                           stop=False)
                        return mm(bank[:, 0:P], c("ident"), c("before"), start=False, stop=not more)

                    def zs(hd):
                        for kb in range(NB):
                            n = hd * NB + kb
                            if due(n - 1):
                                pe.wait_ge(s["z_sp"], n - 1)
                            logits(BK[n % 2], hd, kb, False).then_inc(s["z_mm"], 1)

                    def es_(hd):
                        pe.wait_ge(s["z_sp"], (hd + 1) * NB)
                        for kb in range(NB):
                            n = hd * NB + kb
                            bank = BK[2 + n % 2]
                            if due(n - 1):
                                pe.wait_ge(s["e_exp"], n - 1)
                            logits(bank, hd, kb, True)
                            for jb in range(kb, NB):
                                ins = mm(bank[:, (jb - kb) * P:T - kb * P], c("neg_tri" if jb == kb else "neg_one"),
                                         sp_b[hd % 2][:, OFF[jb]:OFF[jb + 1]], start=False, stop=(jb == NB - 1))
                            ins.then_inc(s["e_mm"], 1)
                        pe.wait_ge(s["e_exp"], (hd + 1) * NB)
                        for qb in range(NB):
                            for kb in range(qb + 1):
                                at_ = OFF[kb] + (qb - kb) * P
                                ins = mm(DB[hd // 2][:, qb * P + hd % 2 * HD:qb * P + hd % 2 * HD + HD],
                                         a_b[hd % 2][:, at_:at_ + P],
                                         tok[:, 2 + hd // 2, kb, hd % 2 * HD:hd % 2 * HD + HD],
                                         start=(kb == 0), stop=(kb == qb))
                        ins.then_inc(s["sbo_mm"], 1)

                    zs(0)
                    for hd in range(HS):
                        if hd + 1 < HS:
                            zs(hd + 1)
                        es_(hd)

                def act_sb(act, s, st):
                    A = nc.scalar.activation

                    def zs(hd):
                        for kb in range(NB):
                            n = hd * NB + kb
                            w = T - kb * P
                            act.wait_ge(s["z_mm"], n + 1)
                            if due(n - 1):
                                act.wait_ge(s["z_sp"], n - 1)
                            A(az[:, n % 2, 0:w], BK[n % 2][:, 0:w], ACT.Abs).then_inc(s["act_step"], 1)
                            act.wait_ge(s["act_step"], st.up("act_step"))
                            A(az[:, n % 2, 0:w], az[:, n % 2, 0:w], ACT.Exp, scale=-1.0).then_inc(s["act_step"], 1)
                            act.wait_ge(s["act_step"], st.up("act_step"))
                            A(az[:, n % 2, 0:w], az[:, n % 2, 0:w], ACT.Ln, bias=1.0).then_inc(s["z_ln"], 1)
                            act.wait_ge(s["z_ln"], st.up("z_ln"))

                    zs(0)
                    for hd in range(HS):
                        if hd + 1 < HS:
                            zs(hd + 1)
                        for kb in range(NB):
                            n = hd * NB + kb
                            w = T - kb * P
                            act.wait_ge(s["e_mm"], n + 1)
                            if due(hd - 1):
                                act.wait_ge(s["sbo_mm"], hd - 1)
                            A(a_b[hd % 2][:, OFF[kb]:OFF[kb + 1]], BK[2 + n % 2][:, 0:w], ACT.Exp)\
                                .then_inc(s["e_exp"], 1)
                            act.wait_ge(s["e_exp"], st.up("e_exp"))

                def dve_sb(dve, s, st):
                    v = nc.vector

                    def soft(n):
                        hd, kb = divmod(n, NB)
                        w = T - kb * P
                        dve.wait_ge(s["z_ln"], n + 1)
                        if due((hd - 1) * NB):
                            dve.wait_ge(s["e_mm"], (hd - 1) * NB)
                        v.scalar_tensor_tensor(sp_b[hd % 2][:, OFF[kb]:OFF[kb + 1]], BK[n % 2][:, 0:w], 0.0,
                                               az[:, n % 2, 0:w], ALU.max, ALU.add).then_inc(s["z_sp"], 1)
                        dve.wait_ge(s["z_sp"], st.up("z_sp"))

                    for n in range(HS * NB):
                        soft(n)
                    for p_ in range(2):
                        dve.wait_ge(s["sbo_mm"], 2 * p_ + 2)
                        v.tensor_copy(o_all[:, :, 768 + p_ * P:768 + (p_ + 1) * P],
                                      DB[p_][:, :].rearrange("p (b f) -> p b f", b=NB)).then_inc(s["sb_done"], 1)
                        dve.wait_ge(s["sb_done"], st.up("sb_done"))

                dl = Layout(nc, x_at, 24576)
                xab = [[dl(f"x{'ab'[i]}{k}", [P, 2, 32, 8]) for i in range(2)] for k in range(2)]
                hid = dl("hid", [P, 2, 2, 32])
                kc2 = dl("kc2", [P, 2, 32])
                vc2 = dl("vc2", [P, P])
                sc = dl("sc", [P, HN, 32])
                et = dl("et", [32, HN * P])
                prob = dl("prob2", [P, T])
                pt = dl("pt2", [P, T])
                small_n = dl("small_n", [P, 64])
                mx, negm, den, wgt = (small_n[:, n:n + 12] for n in (0, 12, 24, 42))
                den = small_n[:, 24:42]
                wgt = small_n[:, 42:60]
                prob = [prob, dl("prob3", [P, T])]
                pt = [pt, Layout(nc, gbuf_at + 8192, 4096)("pt3", [P, T])]
                o_n = z_t[:, 0, 0:384]
                o_m = z_t[:, 1, 0:384]

                def pe_nsa(pe, s, st):
                    mm, tr = nc.tensor.matmul, nc.tensor.transpose
                    for k in range(2):
                        src = roped[:, 0, :] if k == 0 else vc_t[:, :]
                        for gr in range(2):
                            mm(BK[2 * k + gr][:, :], c(f"both{gr}"), src, start=True, stop=True)\
                                .then_inc(s["dup_mm"], 1)
                    pe.wait_ge(s["w1_in"], 32)
                    for k in range(2):
                        pe.wait_ge(s["dup_ready"], 8 * (k + 1))
                        for lp in range(16):
                            i, sh = (0, 0) if lp < 8 else (1, 1)
                            ins = mm(BK[4][:, 64 * k:64 * k + 62], (w1k, w1v)[k][:, lp, :],
                                     xab[k][i][:, :, sh:sh + NCMP, lp % 8], start=(lp == 0), stop=(lp == 15))
                        ins.then_inc(s["hid_mm"], 1)
                    pe.wait_ge(s["hid"], 2)
                    for gr in range(2):
                        mm(STAT[gr * HD:gr * HD + HD, 0:NCMP], g("w2_k"), hid[:, 0, gr, 0:NCMP], start=True,
                           stop=True)
                        ins = mm(STAT[0:NCMP, 64 + gr * HD:64 + gr * HD + HD], hid[:, 1, gr, 0:NCMP], g("w2_v"),
                                 start=True, stop=True)
                    ins.then_inc(s["cmp_mm"], 1)
                    pe.wait_ge(s["cmp_kv"], 1)

                    def query(h_, qb):
                        return roped[h_ // 3 * HD:h_ // 3 * HD + HD, 3 + h_ % 3, blk_of(qb)]

                    def scores(n):
                        qb, i = divmod(n, 12)
                        kind, h_ = divmod(i, HN)
                        if due(n - 1):
                            pe.wait_ge(s["prob"], n - 1)
                        mm(BK[n % 2][:, 0:(qb + 1) * P], query(h_, qb),
                           roped[h_ // 3 * HD:h_ // 3 * HD + HD, 1 + kind, 0:(qb + 1) * P], start=True, stop=False)
                        mm(BK[n % 2][:, blk_of(qb)], c("ident"), c("causal"), start=False,
                           stop=True).then_inc(s["s_mm"], 1)

                    for qb in range(NB):
                        if due(qb):
                            pe.wait_ge(s["nsa_done"], qb)
                        for r in range(3):
                            ins = mm(DB[0][:, r * 64:r * 64 + 64], roped[:, 3 + r, blk_of(qb)],
                                     kc2[:, :, :].rearrange("p g n -> p (g n)"), start=True, stop=True)
                        ins.then_inc(s["cs_mm"], 1)
                        if qb == 0:
                            scores(0)
                        pe.wait_ge(s["cs_exp"], qb + 1)
                        for h_ in range(HN):
                            bank, col = (DB[0], h_ * P) if h_ < 4 else (STAT, (h_ - 4) * P)
                            ins = tr(bank[0:NCMP, col:col + P], sc[:, h_, 0:NCMP], c("ident"))
                        ins.then_inc(s["ct_mm"], 1)
                        pe.wait_ge(s["ct_ready"], 2 * qb + 2)
                        for h_ in range(HN):
                            ins = mm(BK[3][:, h_ * HD:(h_ + 1) * HD], et[0:NCMP, h_ * P:(h_ + 1) * P],
                                     vc2[0:NCMP, h_ // 3 * HD:h_ // 3 * HD + HD], start=True, stop=True)
                        ins.then_inc(s["co_mm"], 1)
                        for i in range(12):
                            n = qb * 12 + i
                            kind, h_ = divmod(i, HN)
                            if n + 1 < 12 * NB:
                                scores(n + 1)
                            pe.wait_ge(s["prob"], n + 1)
                            if due(n - 1):
                                pe.wait_ge(s["pt_ready"], n - 1)
                            for kb in range(qb + 1):
                                ins = tr((BK[2], DB[1])[n % 2][:, blk_of(kb)], prob[n % 2][:, blk_of(kb)], c("ident"))
                            ins.then_inc(s["pt_mm"], 1)
                            pe.wait_ge(s["pt_ready"], n + 1)
                            for kb in range(qb + 1):
                                ins = mm((BK[4], DB[0])[kind][:, h_ * HD:(h_ + 1) * HD], pt[n % 2][:, blk_of(kb)],
                                         tok[:, kind, kb, h_ // 3 * HD:h_ // 3 * HD + HD], start=(kb == 0),
                                         stop=(kb == qb))
                            ins.then_inc(s["pv_mm"], 1)

                def act_nsa(act, s, st):
                    A = nc.scalar.activation
                    act.wait_ge(s["hid_mm"], 2)
                    for k in range(2):
                        A(hid[:, k, :, 0:NCMP], BK[4][:, 64 * k:64 * k + 62].rearrange("p (g n) -> p g n", g=2),
                          ACT.Silu).then_inc(s["hid"], 1)
                        act.wait_ge(s["hid"], st.up("hid"))
                    for qb in range(NB):
                        act.wait_ge(s["cs_sub"], qb + 1)
                        A(sc[:, :, 0:NCMP], sc[:, :, 0:NCMP], ACT.Exp, scale=HD ** -0.5).then_inc(s["cs_exp"], 1)
                        act.wait_ge(s["cs_exp"], st.up("cs_exp"))
                        for i in range(12):
                            n = qb * 12 + i
                            w = (qb + 1) * P
                            act.wait_ge(s["max_ready"], n + 1)
                            if due(n - 1):
                                act.wait_ge(s["pt_mm"], n - 1)
                            A(prob[n % 2][:, 0:w], BK[n % 2][:, 0:w], ACT.Exp, scale=HD ** -0.5,
                              bias=negm[:, i:i + 1], accum_out=den[:, 6 + i:7 + i]).then_inc(s["prob"], 1)
                            act.wait_ge(s["prob"], st.up("prob"))

                def dve_nsa(dve, s, st):
                    v = nc.vector
                    for k in range(2):
                        pe_ = g(("pe_k", "pe_v")[k])
                        for gr in range(2):
                            dve.wait_ge(s["dup_mm"], 2 * k + gr + 1)
                            src = BK[2 * k + gr][:, :].rearrange("p (n l two) -> p n l two", l=8, two=2)
                            for par in range(2):
                                r = slice(par * HD, par * HD + HD)
                                for i in range(2):
                                    v.tensor_tensor(
                                xab[k][i][r, gr, :, :], src[r, :, :, par],
                                pe_[r, 8 * i:8 * i + 8].unsqueeze(1).to_broadcast([HD, 32, 8]), ALU.add)\
                                        .then_inc(s["dup_ready"], 1)
                                    dve.wait_ge(s["dup_ready"], st.up("dup_ready"))
                    dve.wait_ge(s["cmp_mm"], 1)
                    v.memset(kc2[:, :, :], 0.0).then_inc(s["dve_step"], 1)
                    dve.wait_ge(s["dve_step"], st.up("dve_step"))
                    for gr in range(2):
                        r = slice(gr * HD, gr * HD + HD)
                        v.tensor_copy(kc2[r, gr, 0:NCMP], STAT[r, 0:NCMP]).then_inc(s["dve_step"], 1)
                        dve.wait_ge(s["dve_step"], st.up("dve_step"))
                    v.tensor_copy(vc2[0:NCMP, :], STAT[0:NCMP, 64:192]).then_inc(s["cmp_kv"], 1)
                    dve.wait_ge(s["cmp_kv"], st.up("cmp_kv"))

                    def turn_back(n):
                        w = (n // 12 + 1) * P
                        dve.wait_ge(s["pt_mm"], n + 1)
                        if due(n - 1):
                            dve.wait_ge(s["pv_mm"], n - 1)
                        v.tensor_copy(pt[n % 2][:, 0:w], (BK[2], DB[1])[n % 2][:, 0:w]).then_inc(s["pt_ready"], 1)
                        dve.wait_ge(s["pt_ready"], st.up("pt_ready"))

                    heads = lambda x: x.rearrange("p (h d) -> p h d", h=HN)
                    for qb in range(NB):
                        dve.wait_ge(s["cs_mm"], qb + 1)
                        mask = c("cmp_mask")[:, qb * NCMP:(qb + 1) * NCMP].unsqueeze(1).to_broadcast([P, 3, NCMP])
                        scv = sc[:, :, 0:NCMP]
                        for gr in range(2):
                            view = DB[0][:, 0:192].rearrange("p (r g n) -> p r g n", r=3, g=2)[:, :, gr, 0:NCMP]
                            v.tensor_tensor(sc[:, 3 * gr:3 * gr + 3, 0:NCMP], view, mask, ALU.add)\
                                .then_inc(s["dve_step"], 1)
                            dve.wait_ge(s["dve_step"], st.up("dve_step"))
                        v.tensor_reduce(mx[:, 0:HN], scv, AX_X, ALU.max).then_inc(s["dve_step"], 1)
                        dve.wait_ge(s["dve_step"], st.up("dve_step"))
                        v.tensor_tensor(scv, scv, col_bc(mx[:, 0:HN], [P, HN, NCMP]), ALU.subtract)\
                            .then_inc(s["cs_sub"], 1)
                        dve.wait_ge(s["cs_sub"], st.up("cs_sub"))
                        dve.wait_ge(s["cs_exp"], qb + 1)
                        v.tensor_reduce(den[:, 0:HN], scv, AX_X, ALU.add).then_inc(s["dve_step"], 1)
                        dve.wait_ge(s["dve_step"], st.up("dve_step"))
                        dve.wait_ge(s["ct_mm"], qb + 1)
                        v.tensor_copy(et[0:NCMP, 0:512], DB[0][0:NCMP, :]).then_inc(s["ct_ready"], 1)
                        dve.wait_ge(s["ct_ready"], st.up("ct_ready"))
                        v.tensor_copy(et[0:NCMP, 512:768], STAT[0:NCMP, 0:256]).then_inc(s["ct_ready"], 1)
                        dve.wait_ge(s["ct_ready"], st.up("ct_ready"))
                        for i in range(12):
                            n = qb * 12 + i
                            w = (qb + 1) * P
                            dve.wait_ge(s["s_mm"], n + 1)
                            v.tensor_reduce(mx[:, i:i + 1], BK[n % 2][:, 0:w], AX_X, ALU.max)\
                                .then_inc(s["dve_step"], 1)
                            dve.wait_ge(s["dve_step"], st.up("dve_step"))
                            v.tensor_scalar(negm[:, i:i + 1], mx[:, i:i + 1], -HD ** -0.5, None, ALU.mult)\
                                .then_inc(s["max_ready"], 1)
                            dve.wait_ge(s["max_ready"], st.up("max_ready"))
                            if i:
                                turn_back(n - 1)
                        turn_back(qb * 12 + 11)
                        dve.wait_ge(s["prob"], (qb + 1) * 12)
                        v.reciprocal(wgt, den).then_inc(s["dve_step"], 1)
                        dve.wait_ge(s["dve_step"], st.up("dve_step"))
                        v.tensor_tensor(wgt, wgt, gate_w[:, qb, :], ALU.mult).then_inc(s["dve_step"], 1)
                        dve.wait_ge(s["dve_step"], st.up("dve_step"))
                        v.tensor_scalar(wgt[:, 0:HN], wgt[:, 0:HN], c("cmp_any")[:, qb:qb + 1], None, ALU.mult)\
                            .then_inc(s["dve_step"], 1)
                        dve.wait_ge(s["dve_step"], st.up("dve_step"))
                        dve.wait_ge(s["pv_mm"], (qb + 1) * 12)
                        w3 = lambda k: col_bc(wgt[:, HN * k:HN * k + HN], [P, HN, HD])
                        v.tensor_tensor(heads(o_n), heads(BK[3][:, 0:384]), w3(0), ALU.mult)\
                            .then_inc(s["dve_step"], 1)
                        dve.wait_ge(s["dve_step"], st.up("dve_step"))
                        v.tensor_tensor(heads(o_m), heads(BK[4][:, 0:384]), w3(1), ALU.mult)\
                            .then_inc(s["dve_step"], 1)
                        dve.wait_ge(s["dve_step"], st.up("dve_step"))
                        v.tensor_tensor(o_n, o_n, o_m, ALU.add).then_inc(s["dve_step"], 1)
                        dve.wait_ge(s["dve_step"], st.up("dve_step"))
                        v.tensor_tensor(heads(o_m), heads(DB[0][:, 0:384]), w3(2), ALU.mult)\
                            .then_inc(s["dve_step"], 1)
                        dve.wait_ge(s["dve_step"], st.up("dve_step"))
                        v.tensor_tensor(o_all[:, qb, 384:768], o_n, o_m, ALU.add).then_inc(s["nsa_done"], 1)
                        dve.wait_ge(s["nsa_done"], st.up("nsa_done"))

                hsq = Layout(nc, x_at, 32768)("hsq", [P, NB, 640])
                hsum = tiny[:, 200:240]

                def act_heads(act, s, st):
                    act.wait_ge(s["nsa_done"], NB)
                    act.wait_ge(s["sb_done"], 2)
                    nc.scalar.activation(hsq[:, :, :], o_all[:, :, 384:1024], ACT.Square).then_inc(s["hn_sq"], 1)
                    act.wait_ge(s["hn_sq"], st.up("hn_sq"))
                    act.wait_ge(s["hn_red"], 1)
                    nc.scalar.activation(hsum, hsum, ACT.Sqrt, scale=1.0 / HD, bias=c("eps"))\
                        .then_inc(s["hn_root"], 1)
                    act.wait_ge(s["hn_root"], st.up("hn_root"))
                    for q in range(DC):
                        act.wait_ge(s["o_mm"], q + 1)
                        nc.scalar.activation(fh[:, q, :], BK[q % 2][:, :], ACT.Copy).then_inc(s["mix_hi"], 1)
                        act.wait_ge(s["mix_hi"], st.up("mix_hi"))

                def dve_heads(dve, s, st):
                    v = nc.vector
                    dve.wait_ge(s["hn_sq"], 1)
                    v.tensor_reduce(hsum.rearrange("p (b h) -> p b h", b=NB),
                                    hsq[:, :, :].rearrange("p b (h d) -> p b h d", d=HD), AX_X, ALU.add)\
                        .then_inc(s["hn_red"], 1)
                    dve.wait_ge(s["hn_red"], st.up("hn_red"))
                    dve.wait_ge(s["hn_root"], 1)
                    v.reciprocal(hsum, hsum).then_inc(s["dve_step"], 1)
                    dve.wait_ge(s["dve_step"], st.up("dve_step"))
                    for b in range(NB):
                        o3 = o_all[:, b, 384:1024].rearrange("p (h d) -> p h d", d=HD)
                        v.tensor_tensor(o3, o3, col_bc(hsum[:, b * 10:b * 10 + 10], [P, 10, HD]), ALU.mult)\
                            .then_inc(s["dve_step"], 1)
                        dve.wait_ge(s["dve_step"], st.up("dve_step"))
                        v.tensor_tensor(o3[:, 0:6, :], o3[:, 0:6, :],
                                        g("nsa_norm").unsqueeze(1).to_broadcast([P, 6, HD]), ALU.mult)\
                            .then_inc(s["dve_step"], 1)
                        dve.wait_ge(s["dve_step"], st.up("dve_step"))
                        v.tensor_tensor(o3[:, 6:10, :], o3[:, 6:10, :],
                                        g("sb_norm").unsqueeze(1).to_broadcast([P, 4, HD]), ALU.mult)\
                            .then_inc(s["hn_done"], 1)
                        dve.wait_ge(s["hn_done"], st.up("hn_done"))
                    for q in range(DC):
                        dve.wait_ge(s["mix_hi"], q + 1)
                        v.tensor_tensor(fl[:, q, :], BK[q % 2][:, :], fh[:, q, :].bitcast(F32), ALU.subtract)\
                            .then_inc(s["mix_lo"], 1)
                        dve.wait_ge(s["mix_lo"], st.up("mix_lo"))

                def pe_heads(pe, s, st):
                    pe.wait_ge(s["hn_done"], NB)
                    for q in range(DC):
                        if due(q - 1):
                            pe.wait_ge(s["mix_lo"], q - 1)
                        for b in range(NB):
                            ins = nc.tensor.transpose(BK[q % 2][:, blk_of(b)], o_all[:, b, q * P:(q + 1) * P],
                                                      c("ident"))
                        ins.then_inc(s["o_mm"], 1)

                with nc.Fori(0, DEPTH) as layer:
                    with nc.Block() as block:
                        @block.sync
                        def _(sp):
                            sp_weights(sp, s, io["w2"][layer], U2)

                        @block.gpsimd
                        def _(pool):
                            pool_gdn(pool, s, Count())

                        @block.tensor
                        def _(pe):
                            st = Count()
                            mm = nc.tensor.matmul
                            for j in range(DC):
                                pe_stat(pe, s, j, j == 0, j == DC - 1, 0)

                            def post(p_):
                                n = posted[p_]
                                kind, arg = IN2[n]
                                buf = (gbuf, ubuf)[p_ % 2]
                                pe.wait_ge(s["bank"], n + 1)
                                if due(p_ - 1):
                                    pe.wait_ge(s["post_done"], p_ - 1)
                                if kind == "rope":
                                    ins = mm(BK[p_ % 2][:, :], c("swap2"), buf[:, :], start=True, stop=True)
                                else:
                                    for b in range(NB):
                                        ins = nc.tensor.transpose(BK[p_ % 2][:, blk_of(b)], buf[:, blk_of(b)],
                                                                  c("ident"))
                                ins.then_inc(s["post_mm"], 1)

                            for n in range(len(IN2)):
                                pe_unit(pe, s, 0, n, x_hi, x_lo, DC,
                                        (lambda q: ("x_lo", q + 1)) if n == 0 else None)
                                if n - 1 in posted:
                                    post(posted.index(n - 1))
                            post(len(posted) - 1)
                            pe.wait_ge(s["post_done"], len(posted))
                            pe.wait_ge(s["stat_read"], 1)
                            pe_gdn(pe, s, st)
                            pe.wait_ge(s["gdn_done"], GT)
                            pe_sb(pe, s, st)
                            pe.wait_ge(s["sb_done"], 2)
                            pe_nsa(pe, s, st)
                            pe.wait_ge(s["nsa_done"], NB)
                            pe_heads(pe, s, st)
                            pe.wait_ge(s["mix_lo"], DC)
                            for n in range(DC):
                                u = U2_PLE + n // 4
                                if n % 4 == 0:
                                    pe.wait_ge(s["w_lo"], u + 1)
                                if n == 0:
                                    pe.wait_ge(s["p_lo"], 1)
                                if n >= 2:
                                    pe.wait_ge(s[ple_read(n - 2)[0]], ple_read(n - 2)[1])
                                for q in range(2):
                                    col = (n % 4 * 2 + q) * P
                                    w_h, w_l = wh[u % 2][:, col:col + P], wl[u % 2][:, col:col + P]
                                    mm(BK[n % 2][:, :], w_h, p_hi[:, q, :], start=(q == 0), stop=False)
                                    mm(BK[n % 2][:, :], w_h, p_lo[:, q, :], start=False, stop=False)
                                    ins = mm(BK[n % 2][:, :], w_l, p_hi[:, q, :], start=False, stop=(q == 1))
                                ins.then_inc(s[ple_mm(n)[0]], 1)
                                if n > 0:
                                    pe_stat(pe, s, 8 + n - 1, n == 1, False, 1)
                            pe_stat(pe, s, 15, False, True, 1)
                            for n in range(DC):
                                pe_unit(pe, s, 0, U2_OUT + n, f_hi, f_lo, DC,
                                        (lambda q: ("mix_lo", q + 1)) if n == 0 else None)
                                if n > 0:
                                    pe_stat(pe, s, 16 + n - 1, n == 1, False, 2)
                            pe_stat(pe, s, 23, False, True, 2)
                            pe_ffn(pe, s, U2_FFN, 8, 0, 24, 3)
                            for n in range(DC):
                                pe_unit(pe, s, 0, U2_GATE + n, x_hi, x_lo, DC,
                                        (lambda q: ("x_lo", 16 + q + 1)) if n == 0 else None)

                        @block.scalar
                        def _(act):
                            st = Count()
                            A = nc.scalar.activation
                            act.dma_start(small[:, :], io["small2"][layer]).then_inc(s["small_in"], 16)
                            act.wait_ge(s["small_in"], 16)
                            act_split(act, s, st, 0, 0)
                            for j in range(DC):
                                act_tile(act, s, st, j, g("mix"), j)
                                act_square(act, s, st, h[:, j, :], j)
                            act_rstd(act, s, st, 8)
                            for n, (kind, arg) in enumerate(IN2):
                                act_split(act, s, st, 0, n + 1)
                                if kind == "conv":
                                    act.wait_ge(s["bank"], n + 1)
                                    if due(arg):
                                        act.wait_ge(s["conv_done"], arg)
                                    A(ybuf[:, :], cbuf[:, n % 2, 3:], ACT.Copy, scale=gtaps[:, arg, 3:4])\
                                        .then_inc(s["tap0"], 1)
                                    act.wait_ge(s["tap0"], st.up("tap0"))
                                if kind in ("conv", "z") and 1 <= n - 1 <= 9:
                                    act.wait_ge(s["conv_done"], n - 1)
                                    A(qkv[:, n - 2, :], fbuf[:, :] if n % 2 else e_t[:, 0, :], ACT.Silu)\
                                        .then_inc(s["z_ready"], 1)
                                    act.wait_ge(s["z_ready"], st.up("z_ready"))
                            act_gdn(act, s, st)
                            act.wait_ge(s["gdn_done"], GT)
                            act.dma_start(w1k[:, :, :], io["w1c"][layer, 0]).then_inc(s["w1_in"], 16)
                            act.dma_start(w1v[:, :, :], io["w1c"][layer, 1]).then_inc(s["w1_in"], 16)
                            act_sb(act, s, st)
                            act_nsa(act, s, st)
                            act.wait_ge(s["nsa_done"], NB)
                            act.dma_start(p_t[:, :, :], io["p2"][layer]).then_inc(s["p_in"], 16)
                            act_heads(act, s, st)
                            act.wait_ge(s["p_in"], 16)
                            A(p_hi[:, :, :], p_t[:, :, :], ACT.Copy).then_inc(s["p_hi"], 1)
                            act.wait_ge(s["p_hi"], st.up("p_hi"))
                            for n in range(DC):
                                if n % 4 == 0:
                                    act_split(act, s, st, 0, U2_PLE + n // 4 + 1)
                                act.wait_ge(s[ple_read(n)[0]], ple_read(n)[1])
                                act_square(act, s, st, e_t[:, n, :], 8 + n)
                            act_rstd(act, s, st, 16)
                            for n in range(DC):
                                act_split(act, s, st, 0, U2_OUT + n + 1)
                                act.wait_ge(s["bank"], U2_OUT + n + 1)
                                act_tile(act, s, st, n, g("ffn"), 8 + n)
                                act_square(act, s, st, h[:, n, :], 16 + n)
                            act_rstd(act, s, st, 24)
                            act_ffn(act, s, st, U2_FFN, 0, g("gate"), 16, 24, act_conv_pair, CONV_ACT)
                            act_rstd(act, s, st, 32)
                            for n in range(DC):
                                if n < DC - 1:
                                    act_split(act, s, st, 0, U2_GATE + n + 1)
                                act.wait_ge(s["bank"], U2_GATE + n + 1)
                                if due(n):
                                    act.wait_ge(s["out_done"], n)
                                A(sbuf[:, :], (gbuf, ubuf)[n % 2][:, :], ACT.Sigmoid).then_inc(s["sig"], 1)
                                act.wait_ge(s["sig"], st.up("sig"))

                        @block.vector
                        def _(dve):
                            st = Count()
                            v = nc.vector
                            v.memset(cbuf[:, :, 0:3], 0.0).then_inc(s["dve_step"], 1)
                            dve.wait_ge(s["dve_step"], st.up("dve_step"))
                            dve.wait_ge(s["small_in"], 16)
                            dve_split(dve, s, st, 0, 0)
                            for j in range(DC):
                                dve_tile(dve, s, st, j, g("mix"), j)
                            dve_rstd(dve, s, st, 1)

                            def post(p_):
                                kind, arg = IN2[posted[p_]]
                                buf = (gbuf, ubuf)[p_ % 2]
                                if kind == "rope":
                                    v.tensor_tensor(sbuf[:, :], buf[:, :], cos[:, :], ALU.mult)\
                                        .then_inc(s["dve_step"], 1)
                                    dve.wait_ge(s["dve_step"], st.up("dve_step"))
                                    dve.wait_ge(s["post_mm"], p_ + 1)
                                    v.tensor_tensor(buf[:, :], BK[p_ % 2][:, :], sin[:, :], ALU.mult)\
                                        .then_inc(s["dve_step"], 1)
                                    dve.wait_ge(s["dve_step"], st.up("dve_step"))
                                    v.tensor_tensor(roped[:, arg, :], buf[:, :], sbuf[:, :], ALU.add)\
                                        .then_inc(s["post_done"], 1)
                                    dve.wait_ge(s["post_done"], st.up("post_done"))
                                else:
                                    dve.wait_ge(s["post_mm"], p_ + 1)
                                    v.tensor_copy(tok[:, arg, :, :],
                                                  BK[p_ % 2][:, :].rearrange("p (b f) -> p b f", b=NB))\
                                        .then_inc(s["post_done"], 1)
                                    dve.wait_ge(s["post_done"], st.up("post_done"))

                            for n, (kind, arg) in enumerate(IN2):
                                dve_split(dve, s, st, 0, n + 1)
                                dve.wait_ge(s["unit"], n + 1)
                                src = DB[n % 2][:, :]
                                if kind in ("rope", "tok"):
                                    dst = (gbuf, ubuf)[posted.index(n) % 2][:, :]
                                else:
                                    dst = {"rows": rows_t[:, :], "conv": cbuf[:, n % 2, 3:], "z": z_t[:, arg % 3, :],
                                           "vc": vc_t[:, :], "sq": sq_t[:, arg % 2, :],
                                           "sk": sk_t[:, arg % 2, :]}[kind]
                                if kind == "sq":
                                    v.scalar_tensor_tensor(dst, src, HD ** -0.5, rstd[:, :], ALU.mult, ALU.mult)\
                                        .then_inc(s["bank"], 1)
                                    dve.wait_ge(s["bank"], st.up("bank"))
                                else:
                                    v.tensor_tensor(dst, src, rstd[:, :], ALU.mult).then_inc(s["bank"], 1)
                                    dve.wait_ge(s["bank"], st.up("bank"))
                                if kind == "conv":
                                    dve.wait_ge(s["tap0"], arg + 1)
                                    for j in (2, 1):
                                        v.scalar_tensor_tensor(ybuf[:, :], cbuf[:, n % 2, j:j + T],
                                                               gtaps[:, arg, j:j + 1], ybuf[:, :], ALU.mult,
                                                               ALU.add).then_inc(s["dve_step"], 1)
                                        dve.wait_ge(s["dve_step"], st.up("dve_step"))
                                    if due(arg - 1):
                                        dve.wait_ge(s["z_ready"], arg - 1)
                                    out = e_t[:, 0, :] if n % 2 else fbuf[:, :]
                                    v.scalar_tensor_tensor(out, cbuf[:, n % 2, 0:T], gtaps[:, arg, 0:1],
                                                           ybuf[:, :], ALU.mult, ALU.add).then_inc(s["conv_done"], 1)
                                    dve.wait_ge(s["conv_done"], st.up("conv_done"))
                                if n - 1 in posted:
                                    post(posted.index(n - 1))
                            post(len(posted) - 1)
                            dve_gdn(dve, s, st)
                            dve_sb(dve, s, st)
                            dve_nsa(dve, s, st)
                            dve_heads(dve, s, st)
                            dve.wait_ge(s["p_hi"], 1)
                            v.tensor_tensor(p_lo[:, :, :], p_t[:, :, :], p_hi[:, :, :].bitcast(F32),
                                            ALU.subtract).then_inc(s["p_lo"], 1)
                            dve.wait_ge(s["p_lo"], st.up("p_lo"))
                            for n in range(DC):
                                if n % 4 == 0:
                                    dve_split(dve, s, st, 0, U2_PLE + n // 4 + 1)
                                dve.wait_ge(s[ple_mm(n)[0]], ple_mm(n)[1])
                                v.tensor_copy(e_t[:, n, :], BK[n % 2][:, :]).then_inc(s[ple_read(n)[0]], 1)
                                dve.wait_ge(s[ple_read(n)[0]], st.up(ple_read(n)[0]))
                            dve_rstd(dve, s, st, 2)
                            for n in range(DC):
                                v.scalar_tensor_tensor(e_t[:, n, :], e_t[:, n, :], g("ple")[:, n:n + 1],
                                                       rstd[:, :], ALU.mult, ALU.mult).then_inc(s["dve_step"], 1)
                                dve.wait_ge(s["dve_step"], st.up("dve_step"))
                            for n in range(DC):
                                u = U2_OUT + n
                                dve_split(dve, s, st, 0, u + 1)
                                dve.wait_ge(s["unit"], u + 1)
                                v.tensor_tensor(h[:, n, :], DB[u % 2][:, :], h[:, n, :], ALU.add)\
                                    .then_inc(s["bank"], 1)
                                dve.wait_ge(s["bank"], st.up("bank"))
                                dve_tile(dve, s, st, n, g("ffn"), 8 + n)
                            dve_rstd(dve, s, st, 3)
                            dve_ffn(dve, s, st, U2_FFN, 0, g("gate"), 16, 1.0, dve_conv_pair, CONV_DVE)
                            for n in range(DC):
                                u = U2_GATE + n
                                if n < DC - 1:
                                    dve_split(dve, s, st, 0, u + 1)
                                dve.wait_ge(s["unit"], u + 1)
                                if n == 0:
                                    dve_rstd(dve, s, st, 4)
                                buf = (gbuf, ubuf)[n % 2]
                                v.tensor_tensor(buf[:, :], DB[u % 2][:, :], rstd[:, :], ALU.mult)\
                                    .then_inc(s["bank"], 1)
                                dve.wait_ge(s["bank"], st.up("bank"))
                                dve.wait_ge(s["sig"], n + 1)
                                v.tensor_tensor(fbuf[:, :], sbuf[:, :], e_t[:, n, :], ALU.mult)\
                                    .then_inc(s["dve_step"], 1)
                                dve.wait_ge(s["dve_step"], st.up("dve_step"))
                                v.tensor_tensor(h[:, n, :], h[:, n, :], fbuf[:, :], ALU.add)\
                                    .then_inc(s["out_done"], 1)
                                dve.wait_ge(s["out_done"], st.up("out_done"))
                    nc.gpsimd.sem_clear(range(min(ids), max(ids) + 1))
                    nc.all_engine_barrier()


        if which in (0, 1):
            start_block(True, None)
            block1()
            final_norm("final1", io["out"] if which == 1 else None)
        if which in (0, 2):
            start_block(False, None)
            block2()
            final_norm("final2", io["out"])


def tiles(w):
    L, K, N = w.shape
    return w.reshape(L, K // P, P, N // P, P).transpose(0, 3, 2, 1, 4).reshape(L, N // P, P, K // P * P)


def ffn_stream(gate_up, down):
    gu, parts, at = tiles(gate_up), [], 0
    for n in GROUPS:
        for j in range(at, at + n):
            parts += [gu[:, j:j + 1], gu[:, FC + j:FC + j + 1]]
        d = tiles(down[:, at * P:(at + n) * P])
        parts.append(np.pad(d, ((0, 0), (0, 0), (0, 0), (0, UW - n * P))))
        at += n
    return parts


def ple_stream(w):
    t = tiles(w)
    L = t.shape[0]
    return [t.reshape(L, 2, 4, P, 2 * P).transpose(0, 1, 3, 2, 4).reshape(L, 2, P, UW)]


def cols(v):
    return v.reshape(v.shape[0], -1, P).transpose(0, 2, 1)


def rows(v):
    return np.broadcast_to(v[:, None, :], (v.shape[0], P, v.shape[1]))


def layout(i, which):
    i = {k: np.asarray(v) for k, v in i.items()}
    a = {"consts": const_columns()[1]}
    a["x"] = i["x"][0].T.reshape(DC, P, T).transpose(1, 0, 2)
    if which in (0, 1):
        w = i["w_in"]
        qw = w[:, :, :512].reshape(DEPTH, D, 2, 4, HD).transpose(0, 1, 3, 2, 4).reshape(DEPTH, D, 512)
        k, v = w[:, :, 512:640], w[:, :, 640:768]
        ca, cg = tiles(w[:, :, 768:1280]), tiles(w[:, :, 1280:1792])
        conv = np.stack([cg, ca], 2).reshape(DEPTH, 8, P, UW)
        a["w1"] = np.concatenate(
            ffn_stream(i["ffn1_w_gate_up"], i["ffn1_w_down"]) + [tiles(k), tiles(v), tiles(qw), conv]
            + ple_stream(i["w_ple"]) + [tiles(i["w_out"])] + ffn_stream(i["ffn2_w_gate_up"], i["ffn2_w_down"])
            + [tiles(i["w_ple_gate"])], 1)
        taps = i["conv_w"].transpose(0, 2, 1).reshape(DEPTH, CT, P, TAPS).transpose(0, 2, 1, 3).reshape(DEPTH, P, -1)
        a["small1"] = np.concatenate(
            [cols(i[n]) for n in ("ffn1_norm", "mix_norm", "ffn2_norm", "ple_norm", "conv_ln_g", "conv_ln_b",
                                  "conv_b", "conv_out_norm")]
            + [taps, rows(i["sinks"]), rows(i["attn_out_norm"])], 2)
        a["p1"] = i["p"][:, 0].transpose(0, 2, 1).reshape(DEPTH, 2, P, T).transpose(0, 2, 1, 3)
        a["pos1"] = np.broadcast_to(i["positions"], (P, T))
        a["final1"] = cols(i["final_norm"][None])[0]
    if which in (0, 2):
        w = i["w_in_2"]
        edges = np.cumsum([0, 384, 384, 384, 384, 6, 6, 384] + [128] * 6 + [18, 256, 256, 256])
        part = [w[:, :, x:y] for x, y in zip(edges[:-1], edges[1:])]
        gq, gk, gv, gz, ga, gb, nq, kc, vc, ks, vs, kw, vw, gate, sq, sk, sv = part
        rows_w = np.zeros((DEPTH, D, P), w.dtype)
        rows_w[:, :, 0:6], rows_w[:, :, 32:38], rows_w[:, :, 64:82] = ga, gb, gate
        nq = nq.reshape(DEPTH, D, 2, 3, HD).transpose(0, 1, 3, 2, 4).reshape(DEPTH, D, 384)
        a["w2"] = np.concatenate(
            [tiles(x) for x in (rows_w, gq, gk, gv, gz, kc, vc, ks, vs, kw, vw, nq, sq, sk, sv)]
            + ple_stream(i["w_ple_2"]) + [tiles(i["w_out_2"])] + ffn_stream(i["w_up_2"], i["w_down_2"])
            + [tiles(i["w_ple_gate_2"])], 1)
        conv = i["gdn_conv_2"].transpose(0, 2, 1).reshape(DEPTH, 9, P, 4).transpose(0, 2, 1, 3).reshape(DEPTH, P, 36)
        fc = i["ffn_conv_2"].transpose(0, 2, 1).reshape(DEPTH, 2, FC, P, 3).transpose(0, 3, 2, 1, 4)
        head = lambda v: np.pad(v, ((0, 0), (0, P - 6)))[:, :, None]
        pe = lambda v: v.reshape(DEPTH, 16, 2, HD).transpose(0, 2, 3, 1).reshape(DEPTH, P, 16)
        a["small2"] = np.concatenate(
            [cols(i[n]) for n in ("ln_mix_2", "ln_ffn_2", "ln_ple_2", "ple_norm_2")]
            + [conv, fc.reshape(DEPTH, P, 132), head(i["gdn_a_log_2"]), head(i["gdn_dt_bias_2"]),
               rows(i["gdn_norm_2"]), rows(i["nsa_norm_2"]), rows(i["sb_norm_2"]), pe(i["nsa_pe_k_2"]),
               pe(i["nsa_pe_v_2"]), i["nsa_cmp_k_w2_2"], i["nsa_cmp_v_w2_2"]], 2)
        a["w1c"] = np.stack([i[n].reshape(DEPTH, 16, P, P).transpose(0, 2, 1, 3)
                             for n in ("nsa_cmp_k_w1_2", "nsa_cmp_v_w1_2")], 1)
        a["p2"] = i["p_2"][:, 0].transpose(0, 2, 1).reshape(DEPTH, 2, P, T).transpose(0, 2, 1, 3)
        a["pos2"] = np.broadcast_to(i["positions_2"], (P, T))
        a["final2"] = cols(i["ln_final_2"][None])[0]
    return {k: np.ascontiguousarray(v) for k, v in a.items()}


WHICH = 0


def kernel(**inputs):
    import concourse.bacc as _bacc
    from concourse.bass_utils import run_bass_kernel_spmd as _run

    nc = _bacc.Bacc("TRN2", target_bir_lowering=False, num_devices=1)
    arrays = {"in_" + k: v for k, v in layout(inputs, WHICH).items()}
    io = {k[3:]: nc.dram_tensor(k, v.shape, mybir.dt.from_np(v.dtype), kind="ExternalInput").ap()
          for k, v in arrays.items()}
    io["out"] = nc.dram_tensor("out_0", (P, DC, T), F32, kind="ExternalOutput").ap()
    build(nc, io, WHICH)
    r = _run(nc, [arrays], core_ids=[0])
    got = r.results[0]["out_0"]
    return got.transpose(2, 1, 0).reshape(1, T, D)
```
